# Optimizing a Trainium2 kernel written in Bass

```python
import jax, jax.numpy as jnp
from jax import lax
import numpy as np

D_MODEL = 1024
BATCH = 1
SEQ = 1024
DEPTH = 2
DEC_BATCH = 1
DEC_SEQ = 32
PAST_LEN = 128

CHUNK = 64
N_EVEN = (DEPTH + 1) // 2
N_ODD = DEPTH // 2
PLE_DIM = 256
NORM_EPS = 1e-6
NEG_INF = -1e30
CONV_W = 4
A_WIDTH = D_MODEL // 2
A_BLOCKS = 8
A_BLK = A_WIDTH // A_BLOCKS
RG_C = 8.0
B_HEADS = 8
B_KV_HEADS = 2
B_HEAD_DIM = 64
B_GROUPS = B_HEADS // B_KV_HEADS
B_Q = B_HEADS * B_HEAD_DIM
B_KV = B_KV_HEADS * B_HEAD_DIM
WINDOW = 128
WIN_CHUNKS = WINDOW // CHUNK
L0_IN = 2 * A_WIDTH + B_Q + 2 * B_KV
L0_MIX = A_WIDTH + B_Q
C_WIDTH = D_MODEL
C_HEADS = 4
C_HEAD_DIM = C_WIDTH // C_HEADS
C_QK_BLK = 4
L1_IN = 3 * C_WIDTH + 2 * C_HEADS
D_FF = ((8 * D_MODEL + 3 * 256 - 1) // (3 * 256)) * 256

kernel_name = 'hybrid_streaming_rglru_swa_mlstm_step'

def _rmsnorm(x, g):
    x32 = x.astype(jnp.float32)
    y = x32 * lax.rsqrt(jnp.mean(x32 * x32, axis=-1, keepdims=True) + NORM_EPS)
    return (y * g.astype(jnp.float32)).astype(x.dtype)

def _causal_conv(u, buf, w, b):
    t = u.shape[1]
    full = jnp.concatenate([buf.astype(u.dtype), u], axis=1)
    out = b + w[0] * full[:, 0:t]
    for j in range(1, CONV_W):
        out = out + w[j] * full[:, j:j + t]
    return out, full[:, t:]

def _block_diag(x, w):
    nb, bs, _ = w.shape
    xb = x.reshape(x.shape[:-1] + (nb, bs))
    return jnp.einsum('ntgi,gij->ntgj', xb, w).reshape(x.shape)

def _rglru(u, h0, w_r, b_r, w_i, b_i, lam):
    u32 = u.astype(jnp.float32)
    r = jax.nn.sigmoid(_block_diag(u32, w_r) + b_r)
    i = jax.nn.sigmoid(_block_diag(u32, w_i) + b_i)
    log_a = -RG_C * r * jax.nn.softplus(-lam.astype(jnp.float32))
    a = jnp.exp(log_a)
    bx = jnp.sqrt(-jnp.expm1(2.0 * log_a)) * (i * u32)
    bx = bx.at[:, 0].add(a[:, 0] * h0.astype(jnp.float32))

    def comb(left, right):
        a1, b1 = left
        a2, b2 = right
        return a1 * a2, a2 * b1 + b2

    _, h = lax.associative_scan(comb, (a, bx), axis=1)
    return h, h[:, -1]

def _alibi_slopes():
    s = 2.0 ** (-8.0 * jnp.arange(1, B_HEADS + 1, dtype=jnp.float32) / B_HEADS)
    return s.reshape(B_KV_HEADS, B_GROUPS)

def _band(a):
    nc = a.shape[1]
    parts = [jnp.pad(a, ((0, 0), (j, 0), (0, 0), (0, 0), (0, 0)))[:, :nc] for j in range(WIN_CHUNKS, -1, -1)]
    return jnp.concatenate(parts, axis=2)

def _band_bias(nc, slopes):
    c = jnp.arange(nc)[:, None]
    qpos = c * CHUNK + jnp.arange(CHUNK)[None, :]
    back = jnp.repeat(jnp.arange(WIN_CHUNKS, -1, -1), CHUNK)
    kchunk = c - back[None, :]
    kpos = kchunk * CHUNK + jnp.tile(jnp.arange(CHUNK), WIN_CHUNKS + 1)[None, :]
    dist = jnp.abs(qpos[:, :, None] - kpos[:, None, :]).astype(jnp.float32)
    bias = -slopes[None, :, :, None, None] * dist[:, None, None, :, :]
    return jnp.where((kchunk >= 0)[:, None, None, None, :], bias, NEG_INF)

def _attend(q, k, v, bias, sinks):
    s = jnp.einsum('...qkgd,...skd->...kgqs', q.astype(jnp.float32), k.astype(jnp.float32))
    s = s * (B_HEAD_DIM ** -0.5) + bias
    sink = jnp.broadcast_to(sinks.astype(jnp.float32)[:, :, None, None], s.shape[:-1] + (1,))
    p = jax.nn.softmax(jnp.concatenate([s, sink], axis=-1), axis=-1)[..., :-1]
    return jnp.einsum('...kgqs,...skd->...qkgd', p, v.astype(jnp.float32))

def _mix_ab(xn, conv0, h0, cache_k, cache_v, w_in, conv_w, conv_b, w_r, b_r, w_i, b_i, lam, sinks, w_out):
    n_b, t, _ = xn.shape
    proj = xn @ w_in
    g, u, q, k, v = jnp.split(proj, [A_WIDTH, 2 * A_WIDTH, 2 * A_WIDTH + B_Q, 2 * A_WIDTH + B_Q + B_KV], axis=-1)
    uc, new_conv = _causal_conv(u, conv0, conv_w, conv_b)
    hs, h_last = _rglru(uc, h0, w_r, b_r, w_i, b_i, lam)
    y_a = (hs * jax.nn.gelu(g.astype(jnp.float32))).astype(xn.dtype)
    qh = q.reshape(n_b, t, B_KV_HEADS, B_GROUPS, B_HEAD_DIM)
    kh = k.reshape(n_b, t, B_KV_HEADS, B_HEAD_DIM)
    vh = v.reshape(n_b, t, B_KV_HEADS, B_HEAD_DIM)
    slopes = _alibi_slopes()
    sk = sinks.reshape(B_KV_HEADS, B_GROUPS)
    if cache_k is None:
        nc = t // CHUNK
        qb = qh.reshape(n_b, nc, CHUNK, B_KV_HEADS, B_GROUPS, B_HEAD_DIM)
        kb = _band(kh.reshape(n_b, nc, CHUNK, B_KV_HEADS, B_HEAD_DIM))
        vb = _band(vh.reshape(n_b, nc, CHUNK, B_KV_HEADS, B_HEAD_DIM))
        o = _attend(qb, kb, vb, _band_bias(nc, slopes), sk).reshape(n_b, t, B_Q)
        rows = min(WINDOW, t)
        new_k, new_v = kh[:, t - rows:], vh[:, t - rows:]
    else:
        w_rows = cache_k.shape[1]
        kf = jnp.concatenate([cache_k.astype(kh.dtype), kh], axis=1)
        vf = jnp.concatenate([cache_v.astype(vh.dtype), vh], axis=1)
        qpos = PAST_LEN + jnp.arange(t)
        kpos = PAST_LEN - w_rows + jnp.arange(w_rows + t)
        dist = jnp.abs(qpos[:, None] - kpos[None, :]).astype(jnp.float32)
        bias = -slopes[:, :, None, None] * dist[None, None]
        o = _attend(qh, kf, vf, bias, sk).reshape(n_b, t, B_Q)
        new_k, new_v = kh, vh
    y = jnp.concatenate([y_a, o.astype(xn.dtype)], axis=-1) @ w_out
    return y, new_conv, h_last, new_k, new_v

def _mlstm_chunk(carry, xs):
    c_m, n_m, m = carry
    q, k, v, ig, lf = xs
    l = q.shape[1]
    f_cum = jnp.cumsum(lf, axis=1).transpose(0, 2, 1)
    igh = ig.transpose(0, 2, 1)
    causal = jnp.tril(jnp.ones((l, l), dtype=bool))
    dlog = jnp.where(causal, f_cum[..., :, None] - f_cum[..., None, :] + igh[..., None, :], -jnp.inf)
    inter = f_cum + m[..., None]
    m_t = jnp.maximum(inter, dlog.max(axis=-1))
    dw = jnp.exp(dlog - m_t[..., None])
    s = jnp.einsum('nthd,nshd->nhts', q, k) * dw
    w_prev = jnp.exp(inter - m_t)
    num = jnp.einsum('nhts,nshd->nthd', s, v) + w_prev.transpose(0, 2, 1)[..., None] * jnp.einsum('nthd,nhde->nthe', q, c_m)
    den = s.sum(axis=-1) + w_prev * jnp.einsum('nthd,nhd->nht', q, n_m)
    norm = jnp.maximum(jnp.abs(den), jnp.exp(-m_t))
    h = num / norm.transpose(0, 2, 1)[..., None]
    f_last = f_cum[..., -1]
    wlog = f_last[..., None] - f_cum + igh
    m_new = jnp.maximum(f_last + m, wlog.max(axis=-1))
    ws = jnp.exp(wlog - m_new[..., None])
    decay = jnp.exp(f_last + m - m_new)
    c_new = decay[..., None, None] * c_m + jnp.einsum('nhs,nshd,nshe->nhde', ws, k, v)
    n_new = decay[..., None] * n_m + jnp.einsum('nhs,nshd->nhd', ws, k)
    return (c_new, n_new, m_new), h

def _mix_c(xn, conv0, c0, n0, m0, w_in, b_gate, conv_w, conv_b, w_q, w_k, norm_g, w_out):
    n_b, t, _ = xn.shape
    proj = xn @ w_in
    u, v, o, gates = jnp.split(proj, [C_WIDTH, 2 * C_WIDTH, 3 * C_WIDTH], axis=-1)
    gates = gates.astype(jnp.float32) + b_gate.astype(jnp.float32)
    ig = gates[..., :C_HEADS]
    lf = jax.nn.log_sigmoid(gates[..., C_HEADS:])
    uc, new_conv = _causal_conv(u, conv0, conv_w, conv_b)
    uc = jax.nn.silu(uc.astype(jnp.float32))
    hshape = (n_b, t, C_HEADS, C_HEAD_DIM)
    q = _block_diag(uc, w_q).reshape(hshape)
    k = _block_diag(uc, w_k).reshape(hshape) * (C_HEAD_DIM ** -0.5)
    vv = v.astype(jnp.float32).reshape(hshape)
    l = min(t, CHUNK)
    nc = t // l

    def blocks(a):
        return jnp.moveaxis(a.reshape((n_b, nc, l) + a.shape[2:]), 1, 0)

    state0 = (c0.astype(jnp.float32), n0.astype(jnp.float32), m0.astype(jnp.float32))
    (c1, n1, m1), hs = lax.scan(_mlstm_chunk, state0, (blocks(q), blocks(k), blocks(vv), blocks(ig), blocks(lf)))
    h = jnp.moveaxis(hs, 0, 1).reshape(hshape)
    h = jax.nn.sigmoid(o.astype(jnp.float32)).reshape(hshape) * h
    mu = jnp.mean(h, axis=-1, keepdims=True)
    var = jnp.mean(jnp.square(h - mu), axis=-1, keepdims=True)
    h = ((h - mu) * lax.rsqrt(var + NORM_EPS)).reshape(n_b, t, C_WIDTH) * norm_g.astype(jnp.float32)
    y = h.astype(xn.dtype) @ w_out
    return y, new_conv, c1, n1, m1

def _swiglu(x, w_in, w_out):
    gate, up = jnp.split(x @ w_in, 2, axis=-1)
    return (jax.nn.silu(gate) * up) @ w_out

def _trunk(x, p, cache, w):
    n_b = x.shape[0]
    h = x
    a_conv, a_h, b_k, b_v, c_conv, c_c, c_n, c_m = [], [], [], [], [], [], [], []
    for li in range(DEPTH):
        j = li // 2
        hn = _rmsnorm(h, w['norm_mix_g'][li])
        if li % 2 == 0:
            if cache is None:
                conv0 = jnp.zeros((n_b, CONV_W - 1, A_WIDTH), x.dtype)
                h0 = jnp.zeros((n_b, A_WIDTH), jnp.float32)
                ck, cv = None, None
            else:
                conv0, h0 = cache['a_conv'][j], cache['a_h'][j]
                ck, cv = cache['b_k'][j], cache['b_v'][j]
            y, s_conv, s_h, s_k, s_v = _mix_ab(hn, conv0, h0, ck, cv, w['ab_w_in'][j], w['ab_conv_w'][j], w['ab_conv_b'][j], w['ab_w_r'][j], w['ab_b_r'][j], w['ab_w_i'][j], w['ab_b_i'][j], w['ab_lambda'][j], w['ab_sinks'][j], w['ab_w_out'][j])
            a_conv.append(s_conv)
            a_h.append(s_h)
            b_k.append(s_k)
            b_v.append(s_v)
        else:
            if cache is None:
                conv0 = jnp.zeros((n_b, CONV_W - 1, C_WIDTH), x.dtype)
                c0 = jnp.zeros((n_b, C_HEADS, C_HEAD_DIM, C_HEAD_DIM), jnp.float32)
                n0 = jnp.zeros((n_b, C_HEADS, C_HEAD_DIM), jnp.float32)
                m0 = jnp.zeros((n_b, C_HEADS), jnp.float32)
            else:
                conv0, c0, n0, m0 = cache['c_conv'][j], cache['c_C'][j], cache['c_n'][j], cache['c_m'][j]
            y, s_conv, s_c, s_n, s_m = _mix_c(hn, conv0, c0, n0, m0, w['c_w_in'][j], w['c_b_gate'][j], w['c_conv_w'][j], w['c_conv_b'][j], w['c_w_q'][j], w['c_w_k'][j], w['c_norm_g'][j], w['c_w_out'][j])
            c_conv.append(s_conv)
            c_c.append(s_c)
            c_n.append(s_n)
            c_m.append(s_m)
        h = h + y
        h = h + _swiglu(_rmsnorm(h, w['norm_ffn_g'][li]), w['ffn_w_in'][li], w['ffn_w_out'][li])
        h = h + jax.nn.sigmoid(h @ w['ple_w_gate'][li]) * (p[li] @ w['ple_w_proj'][li])
    y_out = _rmsnorm(h, w['final_g'])
    return (y_out, jnp.stack(a_conv), jnp.stack(a_h), jnp.stack(b_k), jnp.stack(b_v), jnp.stack(c_conv), jnp.stack(c_c), jnp.stack(c_n), jnp.stack(c_m))

def setup_inputs(seed: int = 0) -> dict:
    key = jax.random.key(seed)
    ks = iter(jax.random.split(key, 48))

    def nrm(shape, scale):
        return jax.random.normal(next(ks), shape, jnp.float32) * scale

    win_rows = min(WINDOW, PAST_LEN)
    u = jax.random.uniform(next(ks), (N_EVEN, A_WIDTH), jnp.float32, minval=0.9, maxval=0.999)
    s = u ** (1.0 / RG_C)
    lam = jnp.log(s) - jnp.log1p(-s)
    b_gate = jnp.concatenate([nrm((N_ODD, C_HEADS), 0.1), jnp.linspace(3.0, 6.0, C_HEADS)[None, :] + nrm((N_ODD, C_HEADS), 0.1)], axis=-1)
    return {
        'x_prompt': nrm((BATCH, SEQ, D_MODEL), 1.0),
        'x_sample': nrm((DEC_BATCH, DEC_SEQ, D_MODEL), 1.0),
        'cache_a_conv': nrm((N_EVEN, DEC_BATCH, CONV_W - 1, A_WIDTH), 1.0),
        'state_a_h': nrm((N_EVEN, DEC_BATCH, A_WIDTH), 0.5),
        'cache_b_k': nrm((N_EVEN, DEC_BATCH, win_rows, B_KV_HEADS, B_HEAD_DIM), 1.0),
        'cache_b_v': nrm((N_EVEN, DEC_BATCH, win_rows, B_KV_HEADS, B_HEAD_DIM), 1.0),
        'cache_c_conv': nrm((N_ODD, DEC_BATCH, CONV_W - 1, C_WIDTH), 1.0),
        'state_c_C': nrm((N_ODD, DEC_BATCH, C_HEADS, C_HEAD_DIM, C_HEAD_DIM), 0.1),
        'state_c_n': nrm((N_ODD, DEC_BATCH, C_HEADS, C_HEAD_DIM), 0.1),
        'state_c_m': nrm((N_ODD, DEC_BATCH, C_HEADS), 0.5),
        'p_prompt': nrm((DEPTH, BATCH, SEQ, PLE_DIM), 1.0),
        'p_sample': nrm((DEPTH, DEC_BATCH, DEC_SEQ, PLE_DIM), 1.0),
        'norm_mix_g': 1.0 + nrm((DEPTH, D_MODEL), 0.01),
        'norm_ffn_g': 1.0 + nrm((DEPTH, D_MODEL), 0.01),
        'final_g': 1.0 + nrm((D_MODEL,), 0.01),
        'ab_w_in': nrm((N_EVEN, D_MODEL, L0_IN), D_MODEL ** -0.5),
        'ab_conv_w': nrm((N_EVEN, CONV_W, A_WIDTH), CONV_W ** -0.5),
        'ab_conv_b': nrm((N_EVEN, A_WIDTH), 0.01),
        'ab_w_r': nrm((N_EVEN, A_BLOCKS, A_BLK, A_BLK), A_BLK ** -0.5),
        'ab_b_r': nrm((N_EVEN, A_WIDTH), 0.1),
        'ab_w_i': nrm((N_EVEN, A_BLOCKS, A_BLK, A_BLK), A_BLK ** -0.5),
        'ab_b_i': nrm((N_EVEN, A_WIDTH), 0.1),
        'ab_lambda': lam,
        'ab_sinks': nrm((N_EVEN, B_HEADS), 0.5),
        'ab_w_out': nrm((N_EVEN, L0_MIX, D_MODEL), L0_MIX ** -0.5),
        'c_w_in': nrm((N_ODD, D_MODEL, L1_IN), D_MODEL ** -0.5),
        'c_b_gate': b_gate,
        'c_conv_w': nrm((N_ODD, CONV_W, C_WIDTH), CONV_W ** -0.5),
        'c_conv_b': nrm((N_ODD, C_WIDTH), 0.01),
        'c_w_q': nrm((N_ODD, C_WIDTH // C_QK_BLK, C_QK_BLK, C_QK_BLK), C_QK_BLK ** -0.5),
        'c_w_k': nrm((N_ODD, C_WIDTH // C_QK_BLK, C_QK_BLK, C_QK_BLK), C_QK_BLK ** -0.5),
        'c_norm_g': 1.0 + nrm((N_ODD, C_WIDTH), 0.01),
        'c_w_out': nrm((N_ODD, C_WIDTH, D_MODEL), C_WIDTH ** -0.5),
        'ffn_w_in': nrm((DEPTH, D_MODEL, 2 * D_FF), D_MODEL ** -0.5),
        'ffn_w_out': nrm((DEPTH, D_FF, D_MODEL), D_FF ** -0.5),
        'ple_w_proj': nrm((DEPTH, PLE_DIM, D_MODEL), PLE_DIM ** -0.5),
        'ple_w_gate': nrm((DEPTH, D_MODEL, D_MODEL), D_MODEL ** -0.5),
    }

def reference(x_prompt, x_sample, cache_a_conv, state_a_h, cache_b_k, cache_b_v, cache_c_conv, state_c_C, state_c_n, state_c_m, p_prompt, p_sample, norm_mix_g, norm_ffn_g, final_g, ab_w_in, ab_conv_w, ab_conv_b, ab_w_r, ab_b_r, ab_w_i, ab_b_i, ab_lambda, ab_sinks, ab_w_out, c_w_in, c_b_gate, c_conv_w, c_conv_b, c_w_q, c_w_k, c_norm_g, c_w_out, ffn_w_in, ffn_w_out, ple_w_proj, ple_w_gate):
    w = dict(norm_mix_g=norm_mix_g, norm_ffn_g=norm_ffn_g, final_g=final_g, ab_w_in=ab_w_in, ab_conv_w=ab_conv_w, ab_conv_b=ab_conv_b, ab_w_r=ab_w_r, ab_b_r=ab_b_r, ab_w_i=ab_w_i, ab_b_i=ab_b_i, ab_lambda=ab_lambda, ab_sinks=ab_sinks, ab_w_out=ab_w_out, c_w_in=c_w_in, c_b_gate=c_b_gate, c_conv_w=c_conv_w, c_conv_b=c_conv_b, c_w_q=c_w_q, c_w_k=c_w_k, c_norm_g=c_norm_g, c_w_out=c_w_out, ffn_w_in=ffn_w_in, ffn_w_out=ffn_w_out, ple_w_proj=ple_w_proj, ple_w_gate=ple_w_gate)
    (y_prompt, pa_conv, pa_h, pb_k, pb_v, pc_conv, pc_C, pc_n, pc_m) = _trunk(x_prompt, p_prompt, None, w)
    cache = dict(a_conv=cache_a_conv, a_h=state_a_h, b_k=cache_b_k, b_v=cache_b_v, c_conv=cache_c_conv, c_C=state_c_C, c_n=state_c_n, c_m=state_c_m)
    (y_sample, sa_conv, sa_h, sb_k, sb_v, sc_conv, sc_C, sc_n, sc_m) = _trunk(x_sample, p_sample, cache, w)
    return (y_prompt, y_sample, pa_conv, pa_h, pb_k, pb_v, pc_conv, pc_C, pc_n, pc_m, sa_conv, sa_h, sb_k, sb_v, sc_conv, sc_C, sc_n, sc_m)


_drawn_inputs = setup_inputs


def setup_inputs(seed=0):
    import zlib

    import numpy as np

    out = dict(_drawn_inputs(seed))
    spreads = {}
    factors = {'norm_mix_g': 2.767,
     'norm_ffn_g': 4.786,
     'final_g': 32.905,
     'ab_sinks': 32.312,
     'c_conv_b': 2.822,
     'c_norm_g': 64.0,
     'state_c_n': 8.0,
     'state_c_m': 7.332}
    for name, (base, spread) in spreads.items():
        noise = np.random.default_rng([zlib.crc32(name.encode()), seed]).standard_normal(out[name].shape)
        drawn = base * np.exp(spread * noise) if base else spread * noise
        out[name] = __import__('jax').numpy.asarray(drawn.astype(out[name].dtype))
    for name, factor in factors.items():
        out[name] = (out[name] * factor).astype(out[name].dtype)
    return out
```

```python
from contextlib import ExitStack, contextmanager

import numpy as np
import concourse.bass as bass
from concourse import mybir

F32 = mybir.dt.float32
F32R = mybir.dt.float32r
ALU = mybir.AluOpType
ACT = mybir.ActivationFunctionType
AX = mybir.AxisListType
ds = bass.ds

P = 128
D = 1024
KT = D // P
TP, TS = 1024, 32
TOK = TP + TS
NT = 3
TW = TOK // NT
LAST = TP - 2 * TW
EPS = 1e-6
NEG = -1e30
AT = 4
UA = 3 + TP + 3 + TS
CA = UA - 3
SA = TP + 3
HD = 64
SLOTS = 11
NQ = 9
CH = 9
H = 4
HC = 256
UC = 3 + TP + 3 + P
CC = UC - 3
F_TILES = 22
FCH = F_TILES // 2
SLOPE = [2.0 ** -(h + 1) for h in range(8)]

B_IN0, B_OUT0, B_FFN, B_PLE = 14, 8, 6 * FCH, 10
B0_IN = 0
B0_OUT = B0_IN + B_IN0
B0_FFN = B0_OUT + B_OUT0
B0_PLE = B0_FFN + B_FFN
B1_GATE = B0_PLE + B_PLE
B1_U = B1_GATE + 1
B1_PAD = B1_U + 8
B1_VO = B1_PAD + 1
B1_OUT = B1_VO + 16
B1_FFN = B1_OUT + 8
B1_PLE = B1_FFN + B_FFN
NBLK = B1_PLE + B_PLE
NW = 4
NRAW = 2

VEC = {}
_at = 0
for _n, _w in (("g_mix0", 8), ("g_ffn0", 8), ("g_mix1", 8), ("g_ffn1", 8), ("g_fin", 8),
               ("a_w", 16), ("a_b", 4), ("b_r", 4), ("b_i", 4), ("lam", 4), ("h0", 4),
               ("sink", 8), ("c_w", 32), ("c_b", 8), ("c_g", 8), ("b_gate", 1), ("m0", 1), ("eps", 1)):
    VEC[_n] = _at
    _at += _w
NVEC = (_at + 7) // 8 * 8
assert B1_VO % NW in (0, 2)


class Steps:

    def __init__(self, eng, sem):
        self.eng, self.sem, self.base, self.n = eng, sem, 0, 0

    def mark(self, ins):
        ins.then_inc(self.sem, 1)
        self.n += 1

    def wait(self):
        self.eng.wait_ge(self.sem, self.base + self.n)

    def __call__(self, ins):
        self.mark(ins)
        self.wait()

    @contextmanager
    def loop(self, first, end, marks):
        base, n = self.base, self.n
        with self.eng.Fori(first, end) as i:
            self.base, self.n = base + n + (i - first) * marks, 0
            yield i
            assert self.n == marks, (self.n, marks)
        self.base, self.n = base + n + (end - first) * marks, 0


def build(nc, I, O):
    with ExitStack() as ctx:
        base = (nc.sbuf_base + 31) // 32 * 32

        def at(name, off, shape, dt=F32):
            return nc.alloc_sbuf_tensor_at(name, shape, dt, offset=base + 4 * off, align_bytes=4)

        def sem(name):
            return ctx.enter_context(nc.semaphore(name))

        o_wh = NRAW * 1024
        o_wl = o_wh + NW * 1024
        o_xh = o_wl + NW * 1024
        XP = KT * TOK + 96
        o_xl = o_xh + XP
        o_x = o_xl + XP
        m = o_x + KT * TOK
        raw = at("raw", 0, [P, NRAW, KT * P])
        wh = at("wh", o_wh, [P, NW, KT, P], F32R)
        wl = at("wl", o_wl, [P, NW, KT, P], F32R)
        xh_flat = at("xh", o_xh, [P, XP], F32R)
        xl_flat = at("xl", o_xl, [P, XP], F32R)
        xh = xh_flat[:, 0:KT * TOK].rearrange("p (k t) -> p k t", k=KT)
        xl = xl_flat[:, 0:KT * TOK].rearrange("p (k t) -> p k t", k=KT)
        x = at("x", o_x, [P, KT, TOK])
        hh = at("hh", m, [P, 2, 2, TOK], F32R)
        hl = at("hl", m + 4224, [P, 2, 2, TOK], F32R)
        pp = at("pp", m, [P, KT, TOK])
        ph = at("ph", m + 8448, [P, 2, TOK], F32R)
        pl = at("pl", m + 10560, [P, 2, TOK], F32R)
        praw = at("praw", m + 12672, [P, 2, TOK])
        ybuf = at("ybuf", m, [P, KT, TOK])
        tmpa = at("tmpa", m + 14784, [P, 2, TW])
        tmpb = at("tmpb", m + 15488, [P, 2, TW])
        rt = at("rt", m + 16192, [P, TW])
        rstd = at("rstd", m + 16544, [P, TW])
        vecs = at("vecs", m + 16896, [P, NVEC])
        ones = at("ones", m + 16896 + NVEC, [P, P])
        ident = at("ident", m + 16896 + NVEC + 128, [P, P])
        asmall = at("asmall", m + 16896 + NVEC + 256, [P, 8, AT])
        seeds = at("seeds", m + 16896 + NVEC + 288, [P, 24])
        assert NVEC + 256 + 32 + 24 <= 544
        ua = at("ua", m, [P, AT, UA])
        uc = at("uc", m + 4248, [P, CA])
        lr1 = at("lr1", m + 4248 + CA, [P, CA])
        lr2 = at("lr2", m + 4248 + 2 * CA, [P, CA])
        lr3 = at("lr3", m + 4248 + 3 * CA, [P, CA])
        lbd = at("lbd", m + 8484, [P, 2, AT, P])
        dist = at("dist", m + 9508, [P, 3, 2 * P])
        kt = at("kt", m + 10788, [P, SLOTS * P])
        vtok = at("vtok", m + 12196, [P, SLOTS, P])
        vt = at("vt", m + 13604, [P, TOK])
        lr4 = at("lr4", m + 13604, [P, CA])
        ss = at("ss", m, [P, 2, 4, 2 * P])
        pts = at("pts", m + 2048, [P, 8, P])
        otok = at("otok", m + 3072, [P, 4, 2, HD])
        qs = at("qs", m + 3584, [P, 4, P])
        ks = at("ks", m + 4096, [P, 2 * P])
        sm = at("sm", m + 4352, [P, 2, 6, 4])
        ga = at("ga", o_x, [P, 4, TOK])
        qt0 = at("qt0", o_x + 4 * TOK, [P, 4, TOK])
        uu = at("uu", o_x, [P, KT, UC])
        c = o_x + KT * UC
        cbd = at("cbd", c, [P, 2, KT, P])
        sel = at("sel", c + 2048, [4, 4, P])
        arow = at("arow", c + 2560, [4, CH * P])
        cols = at("cols", c + 3712, [P, CH, 4, H])
        decay = at("decay", c + 3856, [P, CH, H])
        cmask = at("cmask", c + 3892, [P, P])
        stage = at("stage", c + 4020, [P, 2, 2 * P])
        cq = at("cq", c + 4532, [P, KT, P])
        ck = at("ck", c + 5556, [P, KT, P])
        vb = at("vb", c + 6580, [P, H, HC + 1])
        ob = at("ob", c + 7608, [P, H, HC])
        cs = at("cs", c + 8632, [P, H, 2, HC + 1])
        kw = at("kw", c + 10688, [P, KT, P])
        dw = at("dw", c + 11712, [P, H, P])
        sw = at("sw", c + 12224, [P, H, P])
        hb = at("hb", c + 12736, [P, H, HC])
        rows = at("rows", c + 6580, [4, 6, CH * P])
        ct = [at("ct0", c + 4532, [P, CC]), at("ct1", c + 10688, [P, CC])]
        assert c + 13760 <= m + 14784
        iq = at("iq", m + 14784, [P, H, HC + 1])
        st = at("st", m + 15812, [P, 128])
        rsmall = at("rsmall", m + 15812 + 128, [4, 64])

        ps = ctx.enter_context(nc.psum_tensor("ps", [P, 8, 512], F32))

        def bank(b, n=TW):
            return ps[:, b, 0:n]

        xsave = nc.dram_tensor("xsave", [P, KT, TOK], F32, kind="Internal").ap()
        vod = nc.dram_tensor("vod", [CH, P, 2 * D], F32, kind="Internal").ap()

        raw_landed = [sem(f"raw_landed{i}") for i in range(NRAW)]
        raw_free = sem("raw_free")
        hi_made = sem("hi_made")
        zero_ready = sem("zero_ready")
        block_done = sem("block_done")
        acc_done = sem("acc_done")
        acc_free = sem("acc_free")
        init_done = sem("init_done")
        const_in = sem("const_in")
        m0_in = sem("m0_in")
        lam_abs = sem("lam_abs")
        lam_exp = sem("lam_exp")
        sp_ready = sem("sp_ready")
        aconv_sent = sem("aconv_sent")
        kv_sent = sem("kv_sent")
        ah_kept = sem("ah_kept")
        ah_sent = sem("ah_sent")
        cconv_sent = sem("cconv_sent")
        m_kept = sem("m_kept")
        m_sent = sem("m_sent")
        c_sent = sem("c_sent")
        y_sent = sem("y_sent")
        x_in = sem("x_in")
        sq_ready = sem("sq_ready")
        sq_used = sem("sq_used")
        ss_done = sem("ss_done")
        rt_ready = sem("rt_ready")
        rstd_ready = sem("rstd_ready")
        xt_ready = sem("xt_ready")
        xh_ready = sem("xh_ready")
        xl_ready = sem("xl_ready")
        dve_step = sem("dve_step")
        act_step = sem("act_step")
        uc_ready = sem("uc_ready")
        gate_done = sem("gate_done")
        gate_out = sem("gate_out")
        et_ready = sem("et_ready")
        iu_done = sem("iu_done")
        sq4_ready = sem("sq4_ready")
        h_ready = sem("h_ready")
        vtr_done = sem("vtr_done")
        v_ready = sem("v_ready")
        y_ready = sem("y_ready")
        yh_ready = sem("yh_ready")
        yl_ready = sem("yl_ready")
        qk_staged = sem("qk_staged")
        s_done = sem("s_done")
        s_read = sem("s_read")
        nm_ready = sem("nm_ready")
        exp_done = sem("exp_done")
        pt_done = sem("pt_done")
        pt_out = sem("pt_out")
        o_done = sem("o_done")
        o_read = sem("o_read")
        ot_done = sem("ot_done")
        oh_ready = sem("oh_ready")
        ol_ready = sem("ol_ready")
        pair_done = sem("pair_done")
        sil_ready = sem("sil_ready")
        h32_ready = sem("h32_ready")
        hh_ready = sem("hh_ready")
        hl_ready = sem("hl_ready")
        down_done = sem("down_done")
        down_added = sem("down_added")
        p_in = sem("p_in")
        ph_ready = sem("ph_ready")
        pl_ready = sem("pl_ready")
        sg_ready = sem("sg_ready")
        ple_added = sem("ple_added")
        x_saved = sem("x_saved")
        c_in = sem("c_in")
        fabs_ready = sem("fabs_ready")
        fexp_ready = sem("fexp_ready")
        rows_log = sem("rows_log")
        rows_ready = sem("rows_ready")
        pads_ready = sem("pads_ready")
        cols_done = sem("cols_done")
        cols_out = sem("cols_out")
        ct_ready = sem("ct_ready")
        silu_done = sem("silu_done")
        stage_full = sem("stage_full")
        stage_out = [sem("stage_out0"), sem("stage_out1")]
        v_in = sem("v_in")
        o_in = sem("o_in")
        qk_done = sem("qk_done")
        qk_out = sem("qk_out")
        ab_done = sem("ab_done")
        dwm_ready = sem("dwm_ready")
        dw_ready = sem("dw_ready")
        st_done = sem("st_done")
        sw_ready = sem("sw_ready")
        ktr_done = sem("ktr_done")
        kw_ready = sem("kw_ready")
        num_done = sem("num_done")
        iq_ready = sem("iq_ready")
        num_read = sem("num_read")
        cup_done = sem("cup_done")
        cup_read = sem("cup_read")
        var_ready = sem("var_ready")
        sd_ready = sem("sd_ready")
        hb_ready = sem("hb_ready")
        htr_done = sem("htr_done")
        ch_ready = sem("ch_ready")
        cl_ready = sem("cl_ready")
        c_zero = sem("c_zero")
        c_swap = sem("c_swap")
        block = ctx.enter_context(nc.Block())

        def vec(name, j=0, n=1):
            return vecs[:, VEC[name] + j:VEC[name] + j + n]

        phases = (("in0", 14, 3 * 14), ("out0", 8, 24), ("proj0", 2, 24), ("gate0", 8, 24),
                  ("g1", 1, 3), ("u1", 8, 24), ("vo1", 16, 72), ("out1", 8, 24),
                  ("proj1", 2, 24), ("gate1", 8, 24))
        DONE0, FREE0, OFF = {}, {}, {}
        nd, nf = 0, 6
        for name, nb, units in phases:
            DONE0[name], FREE0[name], OFF[name] = nd, nf, nf % 6
            ends = {"proj0": 1, "proj1": 1, "vo1": 8}.get(name, nb)
            nd += units - ends
            nf += units
        XLN = {n: KT * NT * j for j, n in enumerate(("mix0", "ffn0", "ple0", "mix1", "ffn1", "ple1"))}
        DA = 24

        def hilo(pe, out, whi, wlo, mhi, mlo, first, last):
            pe.matmul(out, whi, mhi, start=first, stop=False)
            pe.matmul(out, whi, mlo, start=False, stop=False)
            return pe.matmul(out, wlo, mhi, start=False, stop=last)

        @block.sync
        def _(sp):
            with sp.Fori(0, NBLK // NRAW) as i:
                for j in range(NRAW):
                    sp.wait_ge(raw_free, NRAW * i + j + 1)
                    sp.dma_start(raw[:, j, :], I["wstream"][NRAW * i + j]).then_inc(raw_landed[j], 16)

        @block.gpsimd
        def _(pool):
            pool.memset(seeds[:, 0:1], 0.0).then_inc(raw_free, NRAW)
            pool.memset(seeds[:, 1:2], 0.0).then_inc(block_done, NW)
            pool.memset(seeds[:, 2:3], 0.0).then_inc(acc_free, 6)
            pool.memset(seeds[:, 3:4], 0.0).then_inc(down_added, DA)
            pool.memset(seeds[:, 4:5], 0.0).then_inc(silu_done, 2)
            for j, s_ in enumerate((rt_ready, rstd_ready, ss_done, xt_ready, xl_ready, cl_ready, num_read, cup_read,
                                    hb_ready, htr_done, ple_added)):
                pool.memset(seeds[:, 8 + j:9 + j], 0.0).then_inc(s_, 1)
            for j in range(2):
                pool.memset(seeds[:, 20 + j:21 + j], 0.0).then_inc(stage_out[j], 16)
            pool.memset(seeds[:, 6:7], 0.0).then_inc(zero_ready, 1)
            zero = seeds[:, 6:7].to_broadcast([P, KT * P])
            pool.wait_ge(zero_ready, 1)
            with pool.Fori(0, NBLK // NW) as i:
                for j in range(NW):
                    r = j % NRAW
                    pool.wait_ge(raw_landed[r], 16 * (NW // NRAW) * i + 16 * (j // NRAW + 1))
                    pool.wait_ge(block_done, NW * i + j + 1)
                    hi = wh[:, j, :, :].rearrange("p k c -> p (k c)")
                    lo = wl[:, j, :, :].rearrange("p k c -> p (k c)")
                    pool.tensor_tensor(hi, raw[:, r, :], zero, ALU.add).then_inc(hi_made, 1)
                    pool.wait_ge(hi_made, NW * i + j + 1)
                    pool.tensor_tensor(lo, raw[:, r, :], hi.bitcast(F32), ALU.subtract).then_inc(raw_free, 1)

        def split_count(b):
            return b + 1 + NRAW

        def done_count(b):
            return b + 1 + NW

        @block.tensor
        def _(pe):
            def norm(ni):
                with pe.Fori(0, NT) as i:
                    pe.wait_ge(rt_ready, 1 + 3 * ni + i)
                    for k in range(KT):
                        pe.wait_ge(sq_ready, (3 * ni + i) * KT + k + 1)
                        mm = pe.matmul(bank(6), ones[:, :], tmpa[:, k % 2, :], start=(k == 0), stop=(k == KT - 1))
                        mm.then_inc(ss_done if k == KT - 1 else sq_used, 1)

            def dense(slot, b, free, bank0, xl_at=None):
                pe.wait_ge(raw_free, split_count(b))
                for tt in range(NT):
                    if xl_at is not None:
                        pe.wait_ge(xl_ready, 1 + xl_at + KT * (tt + 1))
                    pe.wait_ge(acc_free, free + tt + 1)
                    for k in range(KT):
                        mm = hilo(pe, bank(bank0 + tt), wh[:, slot, k, :], wl[:, slot, k, :],
                                  xh[:, k, tt * TW:(tt + 1) * TW], xl[:, k, tt * TW:(tt + 1) * TW],
                                  k == 0, k == KT - 1)
                    mm.then_inc(acc_done if tt < NT - 1 else block_done, 1)

            def dense_loop(phase, b0, nb, xl_at=None):
                with pe.Fori(0, nb // NW) as i:
                    for j in range(NW):
                        dense((b0 + j) % NW, b0 + NW * i + j, FREE0[phase] - 6 + (NW * i + j) * 3,
                              (OFF[phase] + 3 * j) % 6, xl_at)

            def lru_gates(t):
                pe.wait_ge(uc_ready, t + 1)
                for u in range(6):
                    w, tt = u // 3, u % 3
                    n = 6 * t + u
                    if n >= 2:
                        pe.wait_ge(gate_out, n - 1)
                    pe.matmul(bank(6 + u % 2, 353), lbd[:, w, t, :], uc[:, tt * 353:(tt + 1) * 353],
                              start=True, stop=True).then_inc(gate_done, 1)

            def scores(n, kvh):
                pe.wait_ge(qk_staged, 2 * n + 2)
                if not (isinstance(n, int) and n == 0):
                    pe.wait_ge(s_read, 2 * n + kvh - 1)
                for g in range(4):
                    out = ps[:, 2 * kvh + g // 2, (g % 2) * 256:(g % 2) * 256 + 256]
                    mm = pe.matmul(out, qs[kvh * HD:(kvh + 1) * HD, g, :], ks[kvh * HD:(kvh + 1) * HD, :],
                                   start=True, stop=True)
                mm.then_inc(s_done, 1)

            def attend(n, vslot, nxt):
                for kvh in range(2):
                    pe.wait_ge(exp_done, 2 * n + kvh + 1)
                    pe.wait_ge(pt_out, 2 * n + kvh)
                    for g in range(4):
                        for kk in range(2):
                            j = 2 * g + kk
                            mm = pe.transpose(ps[:, 4 + j // 4, (j % 4) * P:(j % 4 + 1) * P],
                                              ss[:, kvh, g, kk * P:(kk + 1) * P], ident[:, :])
                    mm.then_inc(pt_done, 1)
                    if nxt is not None:
                        scores(nxt, kvh)
                    pe.wait_ge(pt_out, 2 * n + kvh + 1)
                    pe.wait_ge(o_read, 2 * n + kvh)
                    for g in range(4):
                        for kk in range(2):
                            mm = pe.matmul(ps[:, 6, (2 * g + kvh) * HD:(2 * g + kvh + 1) * HD],
                                           pts[:, 2 * g + kk, :], vtok[:, vslot + kk, kvh * HD:(kvh + 1) * HD],
                                           start=(kk == 0), stop=(kk == 1))
                    mm.then_inc(o_done, 1)
                pe.wait_ge(o_read, 2 * n + 2)
                pe.wait_ge(ol_ready, n)
                for g in range(4):
                    mm = pe.transpose(ps[:, 7, g * P:(g + 1) * P],
                                      otok[:, g, :, :].rearrange("p a d -> p (a d)"), ident[:, :])
                mm.then_inc(ot_done, 1)

            def ffn(layer, b0):
                xl_at = XLN[f"ffn{layer}"]
                c0 = FCH * layer

                def up(cx, b, slot0, first=False):
                    for f in range(2):
                        pe.wait_ge(raw_free, split_count(b + 2 * f + 1))
                        for tt in range(NT):
                            pair = 6 * cx + 3 * f + tt
                            if first:
                                pe.wait_ge(xl_ready, 1 + xl_at + KT * (tt + 1))
                            if not (first and f == 0):
                                pe.wait_ge(h32_ready, pair - 2)
                            if not first and f == 0:
                                pe.wait_ge(down_added, DA + 24 * (cx - 2) + 18 + 2 * tt)
                            for w in range(2):
                                slot = (slot0 + 2 * f + w) % NW
                                for k in range(KT):
                                    mm = hilo(pe, bank(2 * tt + w), wh[:, slot, k, :], wl[:, slot, k, :],
                                              xh[:, k, tt * TW:(tt + 1) * TW], xl[:, k, tt * TW:(tt + 1) * TW],
                                              k == 0, k == KT - 1)
                            if tt < 2:
                                mm.then_inc(pair_done, 1)
                            else:
                                mm.then_inc(block_done, 2)

                def down(cx, b, slot0, par, pairs):
                    pe.wait_ge(hl_ready, 6 * (cx + 1))
                    for u in range(24):
                        mo, tt = u // 3, u % 3
                        if u % 12 == 0:
                            pe.wait_ge(raw_free, split_count(b + u // 12))
                        if u < 6:
                            pe.wait_ge(h32_ready, pairs + u // 2 + 1)
                        pe.wait_ge(down_added, DA + 24 * cx + u - 7)
                        slot = (slot0 + u // 12) % NW
                        for kk in range(2):
                            wk = (mo % 4) * 2 + kk
                            mm = hilo(pe, bank(u % 8), wh[:, slot, wk, :], wl[:, slot, wk, :],
                                      hh[:, par, kk, tt * TW:(tt + 1) * TW], hl[:, par, kk, tt * TW:(tt + 1) * TW],
                                      kk == 0, kk == 1)
                        mm.then_inc(block_done if u % 12 == 11 else down_done, 1)

                up(c0, b0, b0 % NW, True)
                with pe.Fori(0, FCH // 2) as i:
                    for j in range(2):
                        cx = c0 + 2 * i + j
                        b = b0 + 4 + 6 * j + 12 * i
                        slot = (b0 + 4 + 6 * j) % NW
                        up(cx + 1, b, slot)
                        down(cx, b + 4, slot, j, 6 * (cx + 1) + 3)
                cx = c0 + FCH - 1
                down(cx, b0 + B_FFN - 2, (b0 + B_FFN - 2) % NW, (FCH - 1) % 2, 6 * cx + 3)

            def ple(layer, b0):
                pe.wait_ge(pl_ready, 2 * (layer + 1))
                pe.wait_ge(raw_free, split_count(b0 + 1))
                pe.wait_ge(down_added, DA + 24 * FCH * (layer + 1))
                for tt in range(NT):
                    for mo in range(KT):
                        u = KT * tt + mo
                        pe.wait_ge(acc_free, FREE0[f"proj{layer}"] - 6 + u + 1)
                        slot = (b0 + mo // 4) % NW
                        for kk in range(2):
                            wk = (mo % 4) * 2 + kk
                            mm = hilo(pe, bank((u + OFF[f"proj{layer}"]) % 6), wh[:, slot, wk, :], wl[:, slot, wk, :],
                                      ph[:, kk, tt * TW:(tt + 1) * TW], pl[:, kk, tt * TW:(tt + 1) * TW],
                                      kk == 0, kk == 1)
                        if u < 23:
                            mm.then_inc(acc_done, 1)
                        else:
                            mm.then_inc(block_done, 2)
                dense_loop(f"gate{layer}", b0 + 2, KT, XLN[f"ple{layer}"])

            pe.wait_ge(const_in, 16 * 3)
            pe.wait_ge(m0_in, 16 * 5)
            norm(0)
            dense_loop("in0", B0_IN, 8, XLN["mix0"])
            for j in range(9):
                n = P if j < 8 else TS
                if j == 0:
                    pe.wait_ge(acc_free, FREE0["in0"] + 3 * 6)
                if j == 4:
                    pe.wait_ge(v_ready, 1)
                if j == 8:
                    pe.wait_ge(v_ready, 2)
                mm = pe.transpose(ps[0:n, 7, (j % 4) * P:(j % 4 + 1) * P], vt[:, j * P:j * P + n], ident[:, :])
                if j in (3, 7, 8):
                    mm.then_inc(vtr_done, 1)
            pe.wait_ge(v_ready, 3)
            for j in range(8, 14):
                dense((B0_IN + j) % NW, B0_IN + j, FREE0["in0"] - 6 + 3 * j, (OFF["in0"] + 3 * j) % 6)
                if 8 <= j < 12:
                    lru_gates(j - 8)
            pe.wait_ge(acc_free, FREE0["in0"] + 42)
            pe.wait_ge(gate_out, 24)
            scores(0, 0)
            scores(0, 1)
            attend(0, 0, 1)
            with pe.Fori(1, NQ - 2) as i:
                attend(i, i, i + 1)
            attend(NQ - 2, NQ - 2, NQ - 1)
            attend(NQ - 1, NQ, None)
            pe.wait_ge(yl_ready, AT)
            pe.wait_ge(ol_ready, NQ)
            dense_loop("out0", B0_OUT, KT)
            norm(1)
            ffn(0, B0_FFN)
            ple(0, B0_PLE)
            norm(2)
            dense(B1_GATE % NW, B1_GATE, FREE0["g1"] - 6, OFF["g1"], XLN["mix1"])
            dense_loop("u1", B1_U, KT)
            pe.wait_ge(rows_ready, 1)
            pe.wait_ge(c_in, 16 * 4)
            for cc in range(CH):
                for q in range(4):
                    r = (0, 5, 4, 1)[q]
                    pe.transpose(ps[:, 6, (cc * 4 + q) * 4:(cc * 4 + q + 1) * 4],
                                 rows[:, r, cc * P:(cc + 1) * P], ident[0:4, 0:4])
            for h in range(H):
                mm = pe.matmul(ps[:, 6, 256 + CH * h:256 + CH * (h + 1)], sel[:, h, :], rsmall[:, 32:32 + CH],
                               start=True, stop=True)
            mm.then_inc(cols_done, 1)
            for half in range(2):
                with pe.Fori(0, 2) as i:
                    for pr in range(2):
                        slot = (2 * pr + B1_VO) % NW
                        pair = 4 * half + 2 * i + pr
                        b = B1_VO + 2 * pair
                        pe.wait_ge(raw_free, split_count(b + 1))
                        for j in range(CH):
                            u = CH * pr + j
                            pe.wait_ge(acc_free, FREE0["vo1"] - 6 + 9 * pair + j + 1)
                            for k in range(KT):
                                mh = xh_flat[:, k * TOK + j * P:k * TOK + (j + 1) * P]
                                ml = xl_flat[:, k * TOK + j * P:k * TOK + (j + 1) * P]
                                out = ps[:, (u + OFF["vo1"]) % 6, 0:2 * P]
                                mm = hilo(pe, out, mh, ml, wh[:, slot:slot + 2, k, :], wl[:, slot:slot + 2, k, :],
                                          k == 0, k == KT - 1)
                            if j < CH - 1:
                                mm.then_inc(acc_done, 1)
                            else:
                                mm.then_inc(block_done, 2)

            def front(n, ucol):
                pe.wait_ge(num_read, 1 + 4 * n)
                for w, b0 in ((1, 2), (0, 6)):
                    if w == 0 and not (isinstance(n, int) and n == 0):
                        pe.wait_ge(cl_ready, n)
                    for t in range(KT):
                        mm = pe.matmul(ps[:, b0 + t // 4, (t % 4) * P:(t % 4 + 1) * P], cbd[:, w, t, :],
                                       uu[:, t, ds(ucol, P)], start=True, stop=True)
                    mm.then_inc(qk_done, 1)
                pe.wait_ge(cup_read, 1 + 8 * n)
                for h in range(H):
                    mm = pe.matmul(ps[:, 4, h * P:(h + 1) * P], sel[:, h, :], arow[:, ds(n * P, P)],
                                   start=True, stop=True)
                mm.then_inc(ab_done, 1)
                pe.wait_ge(qk_out, 2 * n + 1)
                for t in range(KT):
                    mm = pe.transpose(ps[:, t // 4, (t % 4) * P:(t % 4 + 1) * P], ck[:, t, :], ident[:, :])
                mm.then_inc(ktr_done, 1)
                pe.wait_ge(qk_out, 2 * n + 2)
                for h in range(H):
                    for dk in range(2):
                        mm = pe.matmul(ps[:, 5, h * P:(h + 1) * P], ck[:, 2 * h + dk, :], cq[:, 2 * h + dk, :],
                                       start=(dk == 0), stop=(dk == 1))
                mm.then_inc(st_done, 1)

            def transpose_h(n):
                pe.wait_ge(hb_ready, 1 + 4 * n + 4)
                for t in range(KT):
                    mm = pe.transpose(ps[:, 6 + t // 4, (t % 4) * P:(t % 4 + 1) * P],
                                      hb[:, t // 2, (t % 2) * P:(t % 2 + 1) * P], ident[:, :])
                mm.then_inc(htr_done, 1)

            def chunk(n, last):
                pe.wait_ge(v_in, 16 * (n + 1))
                pe.wait_ge(sw_ready, n + 1)
                for h in range(H):
                    if h >= 2:
                        pe.wait_ge(num_read, 1 + 4 * n + h - 1)
                    b0 = (6, 2)[h % 2]
                    for dk in range(2):
                        pe.matmul(bank(b0 + 1, HC + 1), cq[:, 2 * h + dk, :], cs[:, h, dk, :],
                                  start=(dk == 0), stop=(dk == 1))
                    pe.matmul(bank(b0, HC + 1), sw[:, h, :], vb[:, h, :], start=True, stop=True).then_inc(num_done, 1)
                if last is not None:
                    pe.wait_ge(num_read, 1 + 4 * n + 3)
                    transpose_h(last)
                pe.wait_ge(kw_ready, 4 * n + 4)
                for u in range(8):
                    if u >= 4:
                        pe.wait_ge(cup_read, 1 + 8 * n + u - 3)
                    pe.matmul(bank((0, 1, 4, 5)[u % 4], HC + 1), kw[:, u, :], vb[:, u // 2, :],
                              start=True, stop=True).then_inc(cup_done, 1)

            pe.wait_ge(acc_free, FREE0["vo1"] + 72)
            pe.wait_ge(silu_done, KT + 2)
            pe.wait_ge(cols_out, 2)
            pe.wait_ge(c_zero, 2)
            front(0, 0)
            chunk(0, None)
            front(1, P)
            with pe.Fori(1, CH - 2) as i:
                chunk(i, i - 1)
                front(i + 1, i * P + P)
            chunk(CH - 2, CH - 3)
            front(CH - 1, TP + 3)
            pe.wait_ge(c_swap, 16)
            chunk(CH - 1, CH - 2)
            pe.wait_ge(num_read, 1 + 4 * CH)
            pe.wait_ge(cl_ready, CH)
            transpose_h(CH - 1)
            pe.wait_ge(cl_ready, 1 + CH)
            dense_loop("out1", B1_OUT, KT)
            norm(3)
            ffn(1, B1_FFN)
            ple(1, B1_PLE)
            norm(4)

        @block.vector
        def _(dve):
            step = Steps(dve, dve_step)

            def norm(ni):
                with dve.Fori(0, NT) as i:
                    g = 3 * ni + i
                    dve.wait_ge(rt_ready, 1 + g + 1)
                    dve.wait_ge(xt_ready, 1 + KT * g)
                    dve.reciprocal(rstd[:, :], rt[:, :]).then_inc(rstd_ready, 1)
                    dve.wait_ge(rstd_ready, 1 + g + 1)
                    gname = ("g_mix0", "g_ffn0", "g_mix1", "g_ffn1")[ni]
                    base_h = XLN[("mix0", "ffn0", "mix1", "ffn1")[ni]]

                    def low(k):
                        dve.wait_ge(xh_ready, base_h + KT * i + k + 1)
                        dve.tensor_tensor(xl[:, k, ds(i * TW, TW)], tmpb[:, k % 2, :],
                                          xh[:, k, ds(i * TW, TW)].bitcast(F32), ALU.subtract).then_inc(xl_ready, 1)

                    for k in range(KT):
                        dve.wait_ge(xl_ready, 1 + base_h + KT * i + max(k - 1, 0))
                        dve.scalar_tensor_tensor(tmpb[:, k % 2, :], x[:, k, ds(i * TW, TW)], vec(gname, k),
                                                 rstd[:, :], ALU.mult, ALU.mult).then_inc(xt_ready, 1)
                        if k >= 1:
                            low(k - 1)
                    low(KT - 1)

            def unit_wait(tt, done, b):
                if tt < NT - 1:
                    dve.wait_ge(acc_done, done)
                else:
                    dve.wait_ge(block_done, done_count(b))

            def add_loop(phase, b0):
                with dve.Fori(0, KT // NW) as i:
                    for j in range(NW):
                        for tt in range(NT):
                            n = NW * i + j
                            unit_wait(tt, DONE0[phase] + 2 * n + tt + 1, b0 + n)
                            xs = x[:, ds(n, 1), tt * TW:(tt + 1) * TW].rearrange("p a t -> p (a t)")
                            dve.tensor_tensor(xs, bank((OFF[phase] + 3 * j + tt) % 6), xs, ALU.add).then_inc(acc_free, 1)

            def ffn(layer):
                c0 = FCH * layer

                def hidden(cx, par):
                    def low(v):
                        f, tt = v // 3, v % 3
                        dve.wait_ge(hh_ready, 6 * cx + v + 1)
                        dve.tensor_tensor(hl[:, par, f, tt * TW:(tt + 1) * TW], tmpb[:, v % 2, :],
                                          hh[:, par, f, tt * TW:(tt + 1) * TW].bitcast(F32),
                                          ALU.subtract).then_inc(hl_ready, 1)
                    for v in range(6):
                        dve.wait_ge(sil_ready, 6 * cx + v + 1)
                        if not (isinstance(cx, int) and v < 2):
                            dve.wait_ge(hl_ready, 6 * cx + v - 1)
                        dve.tensor_tensor(tmpb[:, v % 2, :], bank(2 * (v % 3) + 1), tmpa[:, v % 2, :],
                                          ALU.mult).then_inc(h32_ready, 1)
                        if v >= 1:
                            low(v - 1)
                    low(5)

                def add(cx, b):
                    for u in range(24):
                        mo, tt = u // 3, u % 3
                        if u % 12 == 11:
                            dve.wait_ge(block_done, done_count(b + u // 12))
                        else:
                            dve.wait_ge(down_done, 22 * cx + u + 1 - u // 12)
                        dve.wait_ge(down_added, DA + 24 * (cx - 1) + u + 1)
                        xs = x[:, mo, tt * TW:(tt + 1) * TW]
                        dve.tensor_tensor(xs, bank(u % 8), xs, ALU.add).then_inc(down_added, 1)

                b0 = (B0_FFN, B1_FFN)[layer]
                dve.wait_ge(xl_ready, 1 + XLN[f"ffn{layer}"] + KT * NT)
                hidden(c0, 0)
                with dve.Fori(0, FCH // 2) as i:
                    for j in range(2):
                        hidden(c0 + 1 + 2 * i + j, (j + 1) % 2)
                        add(c0 + 2 * i + j, b0 + 4 + 12 * i + 6 * j + 4)
                add(c0 + FCH - 1, b0 + B_FFN - 2)

            def ple(layer, b0):
                base_h = XLN[f"ple{layer}"]
                for kk in range(2):
                    dve.wait_ge(ph_ready, 2 * layer + kk + 1)
                    dve.tensor_tensor(pl[:, kk, :], praw[:, kk, :], ph[:, kk, :].bitcast(F32),
                                      ALU.subtract).then_inc(pl_ready, 1)
                for tt in range(NT):
                    for k in range(KT):
                        dve.wait_ge(xh_ready, base_h + KT * tt + k + 1)
                        sl = slice(tt * TW, (tt + 1) * TW)
                        dve.tensor_tensor(xl[:, k, sl], x[:, k, sl], xh[:, k, sl].bitcast(F32),
                                          ALU.subtract).then_inc(xl_ready, 1)
                free = FREE0[f"gate{layer}"]
                dve.wait_ge(acc_free, free)
                with dve.Fori(0, KT // NW) as i:
                    for j in range(NW):
                        for tt in range(NT):
                            n = NW * i + j
                            u = 3 * j + tt
                            dve.wait_ge(sg_ready, 24 * layer + 3 * n + tt + 1)
                            dve.wait_ge(ple_added, 1 + 24 * layer + 3 * n + tt)
                            sl = slice(tt * TW, (tt + 1) * TW)
                            pv = pp[:, ds(n, 1), sl].rearrange("p a t -> p (a t)")
                            xs = x[:, ds(n, 1), sl].rearrange("p a t -> p (a t)")
                            dve.tensor_tensor(tmpb[:, u % 2, :], tmpa[:, u % 2, :], pv, ALU.mult).then_inc(acc_free, 1)
                            dve.wait_ge(acc_free, free + 3 * n + tt + 1)
                            dve.tensor_tensor(xs, tmpb[:, u % 2, :], xs, ALU.add).then_inc(ple_added, 1)

            def log1p(z, e, q, p):
                step(dve.tensor_scalar(z, e, 2.0, None, ALU.add))
                step(dve.reciprocal(z, z))
                step(dve.tensor_tensor(z, z, e, ALU.mult))
                step(dve.tensor_tensor(q, z, z, ALU.mult))
                step(dve.tensor_scalar(p, q, 1.0 / 19.0, None, ALU.mult))
                for d in range(17, 1, -2):
                    step(dve.scalar_tensor_tensor(p, p, 1.0 / d, q, ALU.add, ALU.mult))
                step(dve.scalar_tensor_tensor(p, p, 1.0, z, ALU.add, ALU.mult))

            dve.memset(xh_flat[:, KT * TOK:XP].bitcast(F32), 0.0).then_inc(init_done, 1)
            dve.memset(xl_flat[:, KT * TOK:XP].bitcast(F32), 0.0).then_inc(init_done, 1)
            for t in range(AT):
                dve.memset(ua[:, t, 0:3], 0.0).then_inc(init_done, 1)
            dve.memset(kt[:, 0:P], 0.0).then_inc(init_done, 1)
            dve.memset(kt[:, 10 * P + TS:11 * P], 0.0).then_inc(init_done, 1)
            dve.memset(vtok[:, 0, :], 0.0).then_inc(init_done, 1)
            dve.memset(vtok[:, 10, :], 0.0).then_inc(init_done, 1)
            dve.wait_ge(const_in, 48)
            lam, (e_, z_, q_, p_, sp8, sp4, ab, mx) = vec("lam", 0, 4), [asmall[:, j, :] for j in range(8)]
            dve.scalar_tensor_tensor(ab, lam, -1.0, lam, ALU.mult, ALU.max).then_inc(lam_abs, 1)
            dve.wait_ge(lam_exp, 1)
            log1p(z_, e_, q_, p_)
            step(dve.tensor_scalar(mx, lam, -1.0, 0.0, ALU.mult, ALU.max))
            step(dve.scalar_tensor_tensor(mx, p_, 2.0, mx, ALU.mult, ALU.add))
            dve.tensor_scalar(sp4, mx, 4.0, None, ALU.mult).then_inc(sp_ready, 1)
            dve.tensor_scalar(sp8, mx, -8.0, None, ALU.mult).then_inc(sp_ready, 1)
            norm(0)

            dve.wait_ge(acc_free, FREE0["in0"] + 3 * 8)
            dve.wait_ge(v_ready, 3)
            dve.wait_ge(kv_sent, 48)
            dve.wait_ge(m0_in, 16 * 5)
            dve.wait_ge(init_done, 2 + AT + 4)
            for t in range(AT):
                if t > 0:
                    dve.wait_ge(sq4_ready, t)
                step(dve.tensor_scalar(uc[:, :], ua[:, t, 0:CA], vec("a_w", t), vec("a_b", t), ALU.mult, ALU.add))
                for j in range(1, 4):
                    ins = dve.scalar_tensor_tensor(uc[:, :], ua[:, t, j:j + CA], vec("a_w", 4 * j + t), uc[:, :],
                                                   ALU.mult, ALU.add)
                    if j < 3:
                        step(ins)
                    else:
                        ins.then_inc(uc_ready, 1)
                dve.wait_ge(uc_ready, t + 1)
                dve.wait_ge(gate_out, 6 * t + 6)
                dve.tensor_tensor(lr3[:, :], lr3[:, :], uc[:, :], ALU.mult).then_inc(iu_done, 1)
                dve.wait_ge(et_ready, 2 * t + 2)
                step(dve.tensor_scalar(lr2[:, :], lr2[:, :], 0.5, 0.5, ALU.mult, ALU.add))
                step(dve.scalar_tensor_tensor(lr4[:, :], lr1[:, :], 1.0, lr2[:, :], ALU.add, ALU.mult))
                step(dve.scalar_tensor_tensor(lr4[:, :], lr4[:, :], 2.0, lr2[:, :], ALU.subtract, ALU.mult))
                dve.wait_ge(sq4_ready, t + 1)
                step(dve.scalar_tensor_tensor(lr1[:, :], lr1[:, :], 1.0, lr4[:, :], ALU.subtract, ALU.mult))
                step(dve.scalar_tensor_tensor(lr2[:, :], uc[:, :], -1.0, lr4[:, :], ALU.mult, ALU.mult))
                dve.wait_ge(iu_done, t + 1)
                step(dve.tensor_tensor(lr2[:, :], lr2[:, :], lr3[:, :], ALU.mult))
                dve.wait_ge(aconv_sent, 32)
                step(dve.tensor_tensor_scan(ua[:, t, 0:TP], lr1[:, 0:TP], lr2[:, 0:TP], 0.0, ALU.mult, ALU.add))
                dve.tensor_tensor_scan(ua[:, t, SA:CA], lr1[:, SA:CA], lr2[:, SA:CA], vec("h0", t),
                                       ALU.mult, ALU.add).then_inc(h_ready, 1)
            dve.wait_ge(block_done, done_count(B0_OUT - 1))
            dve.wait_ge(acc_free, FREE0["in0"] + 42)
            dve.wait_ge(h_ready, AT)

            def y_low(t):
                dve.wait_ge(yh_ready, t + 1)
                yb = (lr1, lr2)[t % 2]
                dve.tensor_tensor(xl[:, t, :], yb[:, 0:TOK], xh[:, t, :].bitcast(F32),
                                  ALU.subtract).then_inc(yl_ready, 1)

            for t in range(AT):
                yb = (lr1, lr2)[t % 2]
                if t >= 2:
                    dve.wait_ge(yl_ready, t - 1)
                step(dve.tensor_tensor(yb[:, 0:TP], ua[:, t, 0:TP], ga[:, t, 0:TP], ALU.mult))
                dve.tensor_tensor(yb[:, TP:TOK], ua[:, t, SA:CA], ga[:, t, TP:TOK], ALU.mult).then_inc(y_ready, 1)
                dve.wait_ge(y_ready, t + 1)
                if t >= 1:
                    y_low(t - 1)
            y_low(AT - 1)
            dve.wait_ge(ah_kept, 2)
            dve.wait_ge(yl_ready, AT)

            def before(n, kvh, var):
                dve.wait_ge(s_done, 2 * n + kvh + 1)
                if not (isinstance(n, int) and n == 0):
                    dve.wait_ge(pt_done, 2 * n + kvh - 1)
                for g in range(4):
                    sps = ps[:, 2 * kvh + g // 2, (g % 2) * 256:(g % 2) * 256 + 256]
                    ins = dve.scalar_tensor_tensor(ss[:, kvh, g, :], dist[:, var, :], -8.0 * SLOPE[4 * kvh + g],
                                                   sps, ALU.mult, ALU.add)
                    if g < 3:
                        step.mark(ins)
                    else:
                        ins.then_inc(s_read, 1)
                step.wait()
                dve.wait_ge(s_read, 2 * n + kvh + 1)
                w = [sm[:, kvh, j, :] for j in range(6)]
                step(dve.tensor_reduce(w[0], ss[:, kvh, :, :], AX.X, ALU.max))
                step(dve.scalar_tensor_tensor(w[0], w[0], 0.125, vec("sink", 4 * kvh, 4), ALU.mult, ALU.max))
                step(dve.tensor_scalar(w[1], w[0], -1.0, None, ALU.mult))
                dve.tensor_tensor(w[2], vec("sink", 4 * kvh, 4), w[0], ALU.subtract).then_inc(nm_ready, 1)

            def after(n, kvh):
                w = [sm[:, kvh, j, :] for j in range(6)]
                dve.wait_ge(exp_done, 2 * n + kvh + 1)
                step(dve.tensor_tensor(w[4], w[4], w[3], ALU.add))
                step(dve.reciprocal(w[5], w[4]))
                dve.wait_ge(o_done, 2 * n + kvh + 1)
                dve.wait_ge(ot_done, n)
                ov = ps[:, 6, :].rearrange("p (g a d) -> p g a d", g=4, a=2)[:, :, kvh, :]
                dve.tensor_tensor(otok[:, :, kvh, :], ov,
                                  w[5].rearrange("p (g o) -> p g o", o=1).to_broadcast([P, 4, HD]),
                                  ALU.mult).then_inc(o_read, 1)

            def out_low(n, col, width):
                dve.wait_ge(oh_ready, n + 1)
                ov = ps[:, 7, :].rearrange("p (g t) -> p g t", g=4)[:, :, 0:width]
                dve.tensor_tensor(xl[:, 4:8, ds(col, width)], ov, xh[:, 4:8, ds(col, width)].bitcast(F32),
                                  ALU.subtract).then_inc(ol_ready, 1)

            def attend(n, nxt, var, col, width):
                for kvh in range(2):
                    after(n, kvh)
                    if nxt is not None:
                        before(nxt, kvh, var)
                out_low(n, col, width)

            before(0, 0, 0)
            before(0, 1, 0)
            attend(0, 1, 1, 0, P)
            with step.loop(1, NQ - 2, 2 * (2 + 6)) as i:
                attend(i, i + 1, 1, i * P, P)
            attend(NQ - 2, NQ - 1, 2, (NQ - 2) * P, P)
            attend(NQ - 1, None, None, TP, TS)
            dve.wait_ge(x_in, 16 * 3)
            add_loop("out0", B0_OUT)
            norm(1)
            ffn(0)
            ple(0, B0_PLE)
            norm(2)
            dve.wait_ge(x_saved, 16)
            dve.wait_ge(xl_ready, 1 + XLN["mix1"] + KT * NT)
            dve.memset(uu[:, :, 0:3], 0.0).then_inc(pads_ready, 1)
            dve.memset(uu[:, :, 6 + TOK:UC], 0.0).then_inc(pads_ready, 1)

            R = [rows[:, j, :] for j in range(6)]
            for tt in range(NT):
                unit_wait(tt, DONE0["g1"] + tt + 1, B1_GATE)
                sl = slice(tt * TW, (tt + 1) * TW)
                step.mark(dve.tensor_scalar(rows[:, 0, sl], ps[0:4, tt, 0:TW], vecs[0:4, VEC["b_gate"]:VEC["b_gate"] + 1],
                                            None, ALU.add))
                dve.tensor_scalar(rows[:, 1, sl], ps[32:36, tt, 0:TW], vecs[32:36, VEC["b_gate"]:VEC["b_gate"] + 1],
                                  None, ALU.add).then_inc(acc_free, 1)
            step(dve.memset(rows[:, 0, TOK:CH * P], NEG))
            step(dve.memset(rows[:, 1, TOK:CH * P], 0.0))
            dve.wait_ge(acc_free, FREE0["g1"] + 3)
            dve.scalar_tensor_tensor(R[2], R[1], -1.0, R[1], ALU.mult, ALU.max).then_inc(fabs_ready, 1)
            dve.wait_ge(fexp_ready, 1)
            log1p(R[3], R[2], R[4], R[5])
            step(dve.tensor_scalar(R[1], R[1], 0.0, None, ALU.min))
            step(dve.scalar_tensor_tensor(R[1], R[5], -2.0, R[1], ALU.mult, ALU.add))
            step(dve.memset(R[5], 1.0))
            step(dve.memset(rows[:, 5, 0:CH * P:P], 0.0))
            step(dve.tensor_tensor_scan(R[2], R[5], R[1], 0.0, ALU.mult, ALU.add))
            step(dve.tensor_tensor_scan(rows[:, 3, 0:TP], rows[:, 1, 0:TP], rows[:, 0, 0:TP], 0.0, ALU.add, ALU.max))
            step(dve.tensor_tensor_scan(rows[:, 3, TP:CH * P], rows[:, 1, TP:CH * P], rows[:, 0, TP:CH * P],
                                        vecs[0:4, VEC["m0"]:VEC["m0"] + 1], ALU.add, ALU.max))
            step(dve.tensor_tensor(R[0], R[0], R[2], ALU.subtract))
            step(dve.tensor_tensor(arow[:, :], R[2], R[3], ALU.subtract))
            step(dve.tensor_copy(rsmall[:, 16:24], arow[:, P - 1:TP:P]))
            step(dve.tensor_copy(rsmall[:, 24:25], arow[:, TOK - 1:TOK]))
            step(dve.memset(rsmall[:, 48:49], 0.0))
            step(dve.tensor_copy(rsmall[:, 49:56], rows[:, 3, P - 1:TP - P:P]))
            step(dve.tensor_copy(rsmall[:, 56:57], vecs[0:4, VEC["m0"]:VEC["m0"] + 1]))

            def bc(v):
                return v.rearrange("p (c o) -> p c o", o=1).to_broadcast([4, CH, P])

            def by_chunk(v):
                return v.rearrange("p (c t) -> p c t", c=CH)

            step(dve.tensor_tensor(by_chunk(R[5]), by_chunk(arow[:, :]), bc(rsmall[:, 48:57]), ALU.add))
            step(dve.tensor_tensor(by_chunk(R[1]), by_chunk(R[0]), bc(rsmall[:, 16:25]), ALU.add))
            dve.tensor_tensor(rsmall[:, 32:41], rsmall[:, 16:25], rsmall[:, 48:57], ALU.add).then_inc(rows_log, 1)

            dve.wait_ge(cols_out, 2)
            dve.wait_ge(acc_free, FREE0["u1"] + 24)
            dve.wait_ge(cconv_sent, 32)
            dve.wait_ge(pads_ready, 2)
            dve.wait_ge(c_in, 16 * 4)
            with step.loop(0, KT // 2, 2 * 3) as i:
                for j in range(2):
                    n = 2 * i + j
                    dve.wait_ge(silu_done, n + 1)
                    cv = ct[j][:, :]

                    def uv(o):
                        return uu[:, ds(n, 1), o:o + CC].rearrange("p a t -> p (a t)")

                    def cvec(name, o):
                        return vecs[:, ds(VEC[name] + o + n, 1)]

                    step(dve.tensor_scalar(cv, uv(0), cvec("c_w", 0), cvec("c_b", 0), ALU.mult, ALU.add))
                    for o in range(1, 4):
                        ins = dve.scalar_tensor_tensor(cv, uv(o), cvec("c_w", 8 * o), cv, ALU.mult, ALU.add)
                        if o < 3:
                            step(ins)
                        else:
                            ins.then_inc(ct_ready, 1)
            dve.wait_ge(silu_done, KT + 2)
            dve.memset(cs[:, :, :, :].rearrange("p h k e -> p (h k e)"), 0.0).then_inc(c_zero, 1)
            dve.memset(vb[:, :, HC:HC + 1], 1.0).then_inc(c_zero, 1)
            dve.wait_ge(c_zero, 2)

            def decays(n):
                dve.wait_ge(ab_done, n + 1)
                dve.tensor_tensor(dw[:, :, :], ps[:, 4, :].rearrange("p (h t) -> p h t", h=H),
                                  cmask[:, :].rearrange("p (o t) -> p o t", o=1).to_broadcast([P, H, P]),
                                  ALU.add).then_inc(dwm_ready, 1)

            def weigh(n):
                dve.wait_ge(dw_ready, n + 1)
                dve.wait_ge(st_done, n + 1)
                dve.tensor_tensor(sw[:, :, :].rearrange("p h t -> p (h t)"), ps[:, 5, :],
                                  dw[:, :, :].rearrange("p h t -> p (h t)"), ALU.mult).then_inc(sw_ready, 1)

            def out_low(n, col, width):
                dve.wait_ge(ch_ready, n + 1)
                for t in range(KT):
                    ins = dve.scalar_tensor_tensor(xl[:, t, ds(col, width)],
                                                   ps[:, 6 + t // 4, (t % 4) * P:(t % 4) * P + width], vec("c_g", t),
                                                   xh[:, t, ds(col, width)].bitcast(F32), ALU.mult, ALU.subtract)
                    if t < KT - 1:
                        step.mark(ins)
                    else:
                        ins.then_inc(cl_ready, 1)

            def chunk(n, last, nxt):
                for h in range(H):
                    dve.wait_ge(iq_ready, 4 * n + h + 1)
                    dve.tensor_tensor(iq[:, h, :], bank((6, 2)[h % 2], HC + 1), iq[:, h, :],
                                      ALU.add).then_inc(num_read, 1)
                dve.wait_ge(num_read, 1 + 4 * n + 4)
                step(dve.scalar_tensor_tensor(st[:, 32:36], iq[:, :, HC], -1.0, iq[:, :, HC], ALU.mult, ALU.max))
                step(dve.tensor_tensor(st[:, 32:36], st[:, 32:36],
                                       cols[:, ds(n, 1), 2, :].rearrange("p a h -> p (a h)"), ALU.max))
                step(dve.reciprocal(st[:, 36:40], st[:, 32:36]))
                dve.wait_ge(o_in, 16 * (n + 1))
                dve.wait_ge(htr_done, 1 + n)
                for h in range(H):
                    step.mark(dve.scalar_tensor_tensor(hb[:, h, :], iq[:, h, 0:HC], st[:, 36 + h:37 + h],
                                                       ob[:, h, :], ALU.mult, ALU.mult))

                def update(u):
                    dve.wait_ge(cup_done, 8 * n + u + 1)
                    csv = cs[:, u // 2, u % 2, :]
                    dve.scalar_tensor_tensor(csv, csv, decay_col(n, u // 2), bank((0, 1, 4, 5)[u % 4], HC + 1),
                                             ALU.mult, ALU.add).then_inc(cup_read, 1)

                for u in range(4):
                    update(u)
                if last is not None:
                    out_low(*last)
                for u in range(4, 8):
                    update(u)
                step.wait()
                for h in range(H):
                    step.mark(dve.bn_stats(st[:, 6 * h:6 * h + 6], hb[:, h, :]))
                step.wait()
                if nxt is not None:
                    decays(nxt)
                for h in range(H):
                    dve.bn_aggr(st[:, 24 + 2 * h:26 + 2 * h], st[:, 6 * h:6 * h + 6]).then_inc(var_ready, 1)
                if nxt is not None:
                    weigh(nxt)
                dve.wait_ge(sd_ready, n + 1)
                step(dve.reciprocal(st[:, 44:48], st[:, 40:44]))
                for h in range(H):
                    dve.tensor_scalar(hb[:, h, :], hb[:, h, :], st[:, 24 + 2 * h:25 + 2 * h], st[:, 44 + h:45 + h],
                                      ALU.subtract, ALU.mult).then_inc(hb_ready, 1)

            def decay_col(n, h):
                return decay[:, ds(n, 1), h:h + 1].rearrange("p a h -> p (a h)")

            decays(0)
            weigh(0)
            chunk(0, None, 1)
            with step.loop(1, CH - 2, 3 + 4 + 4 + 1 + 7) as i:
                chunk(i, (i - 1, i * P - P, P), i + 1)
            chunk(CH - 2, (CH - 3, (CH - 3) * P, P), CH - 1)
            dve.wait_ge(c_swap, 16)
            chunk(CH - 1, (CH - 2, (CH - 2) * P, P), None)
            out_low(CH - 1, TP, TS)
            dve.wait_ge(x_in, 16 * 4)
            add_loop("out1", B1_OUT)
            norm(3)
            ffn(1)
            ple(1, B1_PLE)

            dve.wait_ge(ple_added, 1 + 48)
            with dve.Fori(0, NT) as i:
                dve.wait_ge(rt_ready, 1 + 12 + i + 1)
                dve.wait_ge(xt_ready, 1 + KT * (12 + i))
                dve.reciprocal(rstd[:, :], rt[:, :]).then_inc(rstd_ready, 1)
                dve.wait_ge(rstd_ready, 1 + 12 + i + 1)
                for k in range(KT):
                    dve.scalar_tensor_tensor(ybuf[:, k, ds(i * TW, TW)], x[:, k, ds(i * TW, TW)], vec("g_fin", k),
                                             rstd[:, :], ALU.mult, ALU.mult).then_inc(xt_ready, 1)

        @block.scalar
        def _(act):
            def norm(ni):
                with act.Fori(0, NT) as i:
                    g = 3 * ni + i
                    for k in range(KT):
                        n = KT * ni * 3 - 3 * ni + i * (KT - 1)
                        if k >= 2:
                            act.wait_ge(sq_used, n + k - 1)
                        else:
                            act.wait_ge(ss_done, 1 + g)
                        act.activation(tmpa[:, k % 2, :], x[:, k, ds(i * TW, TW)], ACT.Square).then_inc(sq_ready, 1)
                    act.wait_ge(ss_done, 1 + g + 1)
                    act.wait_ge(rstd_ready, 1 + g)
                    act.activation(rt[:, :], bank(6), ACT.Sqrt, bias=vec("eps"), scale=1.0 / D).then_inc(rt_ready, 1)
                    if ni < 4:
                        base_h = XLN[("mix0", "ffn0", "mix1", "ffn1")[ni]]
                        for k in range(KT):
                            act.wait_ge(xt_ready, 1 + KT * g + k + 1)
                            act.activation(xh[:, k, ds(i * TW, TW)], tmpb[:, k % 2, :], ACT.Copy).then_inc(xh_ready, 1)

            def ffn(layer):
                c0 = FCH * layer

                def hidden(cx, b, par, outs):
                    if outs:
                        act.wait_ge(down_added, DA + 24 * (cx - 1))

                    def high(v):
                        f, tt = v // 3, v % 3
                        act.wait_ge(h32_ready, 6 * cx + v + 1)
                        act.activation(hh[:, par, f, tt * TW:(tt + 1) * TW], tmpb[:, v % 2, :],
                                       ACT.Copy).then_inc(hh_ready, 1)
                    for v in range(6):
                        f, tt = v // 3, v % 3
                        if tt < 2:
                            act.wait_ge(pair_done, 4 * cx + 2 * f + tt + 1)
                        else:
                            act.wait_ge(block_done, done_count(b + 2 * f + 1))
                        act.activation(tmpa[:, v % 2, :], bank(2 * tt), ACT.Silu).then_inc(sil_ready, 1)
                        if v >= 1:
                            high(v - 1)
                    high(5)

                b0 = (B0_FFN, B1_FFN)[layer]
                hidden(c0, b0, 0, False)
                with act.Fori(0, FCH // 2) as i:
                    for j in range(2):
                        hidden(c0 + 1 + 2 * i + j, b0 + 4 + 12 * i + 6 * j, (j + 1) % 2, True)

            def ple(layer, b0):
                act.wait_ge(p_in, 16 * (layer + 1))
                for kk in range(2):
                    act.activation(ph[:, kk, :], praw[:, kk, :], ACT.Copy).then_inc(ph_ready, 1)
                act.wait_ge(down_added, DA + 24 * FCH * (layer + 1))
                off = OFF[f"proj{layer}"]
                for tt in range(NT):
                    sl = slice(tt * TW, (tt + 1) * TW)
                    for k in range(KT):
                        act.activation(xh[:, k, sl], x[:, k, sl], ACT.Copy).then_inc(xh_ready, 1)
                    for mo in range(KT):
                        u = KT * tt + mo
                        if u < 23:
                            act.wait_ge(acc_done, DONE0[f"proj{layer}"] + u + 1)
                        else:
                            act.wait_ge(block_done, done_count(b0 + 1))
                        act.activation(pp[:, mo, sl], bank((u + off) % 6), ACT.Copy).then_inc(acc_free, 1)
                with act.Fori(0, KT // NW) as i:
                    for j in range(NW):
                        for tt in range(NT):
                            n = NW * i + j
                            u = 3 * j + tt
                            unit_wait(tt, DONE0[f"gate{layer}"] + 2 * n + tt + 1, b0 + 2 + n)
                            act.wait_ge(acc_free, FREE0[f"gate{layer}"] + 3 * n + tt - 1)
                            act.activation(tmpa[:, u % 2, :], bank((OFF[f"gate{layer}"] + u) % 6),
                                           ACT.Sigmoid).then_inc(sg_ready, 1)

            def unit_wait(tt, done, b):
                if tt < NT - 1:
                    act.wait_ge(acc_done, done)
                else:
                    act.wait_ge(block_done, done_count(b))

            act.dma_start(vecs[:, :], I["vecs"]).then_inc(const_in, 16)
            act.dma_start(x[:, :, :], I["xT"]).then_inc(x_in, 16)
            act.dma_start(ones[:, :], I["ones"]).then_inc(const_in, 16)
            act.dma_start(ident[:, :], I["ident"]).then_inc(const_in, 16)
            act.dma_start(lbd[:, :, :, :], I["lbd"]).then_inc(m0_in, 16)
            act.dma_start(dist[:, :, :], I["dist"]).then_inc(m0_in, 16)
            act.dma_start(ua[:, :, 3 + TP:6 + TP], I["a_conv"]).then_inc(m0_in, 16)
            act.dma_start(kt[:, 9 * P:10 * P], I["kc"]).then_inc(m0_in, 16)
            act.dma_start(vtok[:, 9, :], I["vc"]).then_inc(m0_in, 16)
            act.wait_ge(lam_abs, 1)
            act.activation(asmall[:, 0, :], asmall[:, 6, :], ACT.Exp, scale=-1.0).then_inc(lam_exp, 1)
            act.wait_ge(x_in, 16)
            norm(0)

            def copy_out(j):
                for tt in range(NT):
                    unit_wait(tt, DONE0["in0"] + 2 * j + tt + 1, B0_IN + j)
                    src = bank((OFF["in0"] + 3 * j + tt) % 6)
                    if j < 5:
                        dst, sample = (ua[:, j, :], 6 + TP) if j < 4 else (kt[:, :], 10 * P)
                        off = 3 if j < 4 else P
                        if tt < NT - 1:
                            act.activation(dst[:, off + tt * TW:off + (tt + 1) * TW], src, ACT.Copy).then_inc(acc_free, 1)
                        else:
                            act.activation(dst[:, off + tt * TW:off + TP], src[:, 0:LAST], ACT.Copy)
                            act.activation(dst[:, sample:sample + TS], src[:, LAST:TW], ACT.Copy).then_inc(acc_free, 1)
                        continue
                    sl = slice(tt * TW, (tt + 1) * TW)
                    if j == 5:
                        act.activation(vt[:, sl], src, ACT.Copy).then_inc(acc_free, 1)
                    elif j < 10:
                        act.activation(qt0[:, j - 6, sl], src, ACT.Copy).then_inc(acc_free, 1)
                    else:
                        act.activation(ga[:, j - 10, sl], src, ACT.Gelu_apprx_tanh).then_inc(acc_free, 1)

            def lru(t):
                act.wait_ge(h_ready, t)
                for u in range(6):
                    act.wait_ge(gate_done, 6 * t + u + 1)
                    dst, b = ((lr1, "b_r"), (lr3, "b_i"))[u // 3]
                    sl = slice((u % 3) * 353, (u % 3 + 1) * 353)
                    act.activation(dst[:, sl], bank(6 + u % 2, 353), ACT.Sigmoid, bias=vec(b, t)).then_inc(gate_out, 1)
                act.wait_ge(gate_out, 6 * t + 6)
                act.activation(lr2[:, :], lr1[:, :], ACT.Exp, scale=asmall[:, 4, t:t + 1]).then_inc(et_ready, 1)
                act.activation(lr1[:, :], lr1[:, :], ACT.Tanh, scale=asmall[:, 5, t:t + 1]).then_inc(et_ready, 1)
                act.wait_ge(et_ready, 2 * t + 2)
                act.wait_ge(iu_done, t + 1)
                act.activation(uc[:, :], lr1[:, :], ACT.Sqrt, scale=4.0).then_inc(sq4_ready, 1)

            act.wait_ge(m0_in, 16 * 5)
            act.wait_ge(init_done, 2 + AT + 4)
            for j in range(8):
                copy_out(j)
                if j == 4:
                    act.wait_ge(acc_free, FREE0["in0"] + 15)
                    act.dma_start(O["a_conv_o"][:, :, 0:3], ua[:, :, TP:TP + 3]).then_inc(aconv_sent, 16)
                    act.dma_start(O["a_conv_o"][:, :, 3:6], ua[:, :, UA - 3:UA]).then_inc(aconv_sent, 16)
                    act.dma_start(O["k_o"][:, 0:P], kt[:, TP:TP + P]).then_inc(kv_sent, 16)
                    act.dma_start(O["k_o"][:, P:P + TS], kt[:, 10 * P:10 * P + TS]).then_inc(kv_sent, 16)
                if j == 6:
                    act.wait_ge(acc_free, FREE0["in0"] + 18)
                    act.dma_start(O["v_o"], vt[:, TOK - P - TS:TOK]).then_inc(kv_sent, 16)
            for j in range(3):
                act.wait_ge(vtr_done, j + 1)
                if j < 2:
                    act.activation(vtok[:, 4 * j + 1:4 * j + 5, :].rearrange("p a d -> p (a d)"), ps[:, 7, :],
                                   ACT.Copy).then_inc(v_ready, 1)
                else:
                    act.activation(vtok[0:TS, 10, :], ps[0:TS, 7, 0:P], ACT.Copy).then_inc(v_ready, 1)
            act.wait_ge(sp_ready, 2)
            for j in range(8, 14):
                copy_out(j)
                if 8 <= j < 12:
                    lru(j - 8)
            act.wait_ge(h_ready, AT)
            act.activation(asmall[:, 2, :], ua[:, :, TP - 1], ACT.Copy).then_inc(ah_kept, 1)
            act.activation(asmall[:, 3, :], ua[:, :, CA - 1], ACT.Copy).then_inc(ah_kept, 1)
            act.wait_ge(ah_kept, 2)
            act.dma_start(O["a_h_o"], asmall[:, 2:4, :]).then_inc(ah_sent, 16)
            act.wait_ge(block_done, done_count(B0_OUT - 1))
            for t in range(AT):
                act.wait_ge(y_ready, t + 1)
                act.activation(xh[:, t, :], (lr1, lr2)[t % 2][:, 0:TOK], ACT.Copy).then_inc(yh_ready, 1)
            act.wait_ge(yl_ready, AT)
            act.dma_start(x[:, 0:4, :], I["xT"][:, 0:4, :]).then_inc(x_in, 16)

            def stage_qk(n, col, width, kcol):
                act.wait_ge(s_done, 2 * n)
                act.activation(qs[:, :, 0:width], qt0[:, :, ds(col, width)], ACT.Copy).then_inc(qk_staged, 1)
                act.activation(ks[:, :], kt[:, ds(kcol, 2 * P)], ACT.Copy).then_inc(qk_staged, 1)

            def exps(n, kvh):
                act.wait_ge(nm_ready, 2 * n + kvh + 1)
                act.activation(sm[:, kvh, 3, :], sm[:, kvh, 2, :], ACT.Exp)
                for g in range(4):
                    ins = act.activation(ss[:, kvh, g, :], ss[:, kvh, g, :], ACT.Exp, bias=sm[:, kvh, 1, g:g + 1],
                                         scale=0.125, accum_out=sm[:, kvh, 4, g:g + 1])
                ins.then_inc(exp_done, 1)

            def attend(n, nxt, ncol, nwidth, nkcol, col, width):
                if nxt is not None:
                    stage_qk(nxt, ncol, nwidth, nkcol)
                for kvh in range(2):
                    act.wait_ge(pt_done, 2 * n + kvh + 1)
                    act.wait_ge(o_done, 2 * n + kvh)
                    act.activation(pts[:, :, :].rearrange("p a q -> p (a q)"),
                                   ps[:, 4:6, :].rearrange("p b q -> p (b q)"), ACT.Copy).then_inc(pt_out, 1)
                    if nxt is not None:
                        exps(nxt, kvh)
                act.wait_ge(ot_done, n + 1)
                act.activation(xh[:, 4:8, ds(col, width)],
                               ps[:, 7, :].rearrange("p (g t) -> p g t", g=4)[:, :, 0:width],
                               ACT.Copy).then_inc(oh_ready, 1)

            stage_qk(0, 0, P, 0)
            exps(0, 0)
            exps(0, 1)
            attend(0, 1, P, P, P, 0, P)
            with act.Fori(1, NQ - 2) as i:
                attend(i, i + 1, i * P + P, P, i * P + P, i * P, P)
            attend(NQ - 2, NQ - 1, TP, TS, 9 * P, (NQ - 2) * P, P)
            act.wait_ge(qk_staged, 2 * NQ)
            act.dma_start(x[:, 4:8, :], I["xT"][:, 4:8, :]).then_inc(x_in, 16)
            attend(NQ - 1, None, None, None, None, TP, TS)
            act.wait_ge(ol_ready, NQ)
            act.dma_start(praw[:, :, :], I["pT"][0]).then_inc(p_in, 16)
            act.wait_ge(acc_free, FREE0["out0"] + 24)
            norm(1)
            ffn(0)
            ple(0, B0_PLE)

            act.wait_ge(ple_added, 1 + 24)
            act.dma_start(xsave, x[:, :, :]).then_inc(x_saved, 16)
            act.dma_start(cbd[:, :, :, :], I["cbd"]).then_inc(c_in, 16)
            act.dma_start(sel[:, :, :], I["sel"]).then_inc(c_in, 16)
            act.dma_start(cmask[:, :], I["cmask"]).then_inc(c_in, 16)
            norm(2)
            act.wait_ge(x_saved, 16)
            act.wait_ge(xl_ready, 1 + XLN["mix1"] + KT * NT)
            act.dma_start(uu[:, :, 3 + TP:6 + TP], I["c_conv"]).then_inc(c_in, 16)
            act.wait_ge(c_in, 64)
            act.wait_ge(pads_ready, 2)

            def u_out(n, j):
                for tt in range(NT):
                    unit_wait(tt, DONE0["u1"] + 2 * n + tt + 1, B1_U + n)
                    src = bank((OFF["u1"] + 3 * j + tt) % 6)
                    dst = uu[:, ds(n, 1), :].rearrange("p a t -> p (a t)")
                    if tt < NT - 1:
                        act.activation(dst[:, 3 + tt * TW:3 + (tt + 1) * TW], src, ACT.Copy).then_inc(acc_free, 1)
                    else:
                        act.activation(dst[:, 3 + tt * TW:3 + TP], src[:, 0:LAST], ACT.Copy)
                        act.activation(dst[:, 6 + TP:6 + TOK], src[:, LAST:TW], ACT.Copy).then_inc(acc_free, 1)

            def row_exps():
                act.wait_ge(rows_log, 1)
                act.activation(rsmall[:, 60:62], rows[:, 3, TP - 1:TOK:TS], ACT.Copy).then_inc(m_kept, 1)
                act.wait_ge(m_kept, 1)
                act.dma_start(O["m_o"], rsmall[:, 60:62]).then_inc(m_sent, 16)
                act.activation(rows[:, 4, :], rows[:, 3, :], ACT.Exp, scale=-1.0)
                act.activation(rows[:, 5, :], rows[:, 5, :], ACT.Exp)
                act.activation(rows[:, 1, :], rows[:, 1, :], ACT.Exp)
                act.activation(rsmall[:, 32:41], rsmall[:, 32:41], ACT.Exp).then_inc(rows_ready, 1)

            act.wait_ge(fabs_ready, 1)
            act.activation(rows[:, 2, :], rows[:, 2, :], ACT.Exp, scale=-1.0).then_inc(fexp_ready, 1)
            with act.Fori(0, KT // NW) as i:
                for j in range(NW):
                    u_out(NW * i + j, j)
            act.wait_ge(acc_free, FREE0["u1"] + 24)
            act.activation(seeds[:, 5:6], seeds[:, 0:1], ACT.Copy).then_inc(block_done, 1)
            act.dma_start(O["c_conv_o"][:, :, 0:3], uu[:, :, TP:TP + 3]).then_inc(cconv_sent, 16)
            act.dma_start(O["c_conv_o"][:, :, 3:6], uu[:, :, 3 + TOK:6 + TOK]).then_inc(cconv_sent, 16)
            row_exps()
            act.wait_ge(cols_done, 1)
            act.activation(cols[:, :, :, :].rearrange("p c q h -> p (c q h)"), ps[:, 6, 0:CH * 4 * H],
                           ACT.Copy).then_inc(cols_out, 1)
            act.activation(decay[:, :, :].rearrange("p c h -> p h c"),
                           ps[:, 6, 256:256 + CH * H].rearrange("p (h c) -> p h c", h=H), ACT.Copy).then_inc(cols_out, 1)

            def silu(n, j):
                act.wait_ge(ct_ready, n + 1)
                act.activation(uu[:, ds(n, 1), 0:CC].rearrange("p a t -> p (a t)"), ct[j][:, :],
                               ACT.Silu).then_inc(silu_done, 1)

            def vo_out(pair, pr, it, func, j):
                u = CH * pr + j
                if j < CH - 1:
                    act.wait_ge(acc_done, DONE0["vo1"] + 8 * pair + j + 1)
                else:
                    act.wait_ge(block_done, done_count(B1_VO + 2 * pair + 1))
                act.wait_ge(stage_out[u % 2], 16 + 16 * (CH * it + u // 2))
                act.activation(stage[:, u % 2, :], ps[:, (u + OFF["vo1"]) % 6, 0:2 * P], func).then_inc(acc_free, 1)
                act.wait_ge(acc_free, FREE0["vo1"] + CH * pair + j + 1)
                act.dma_start(vod[j, :, ds(pair * 2 * P, 2 * P)], stage[:, u % 2, :]).then_inc(stage_out[u % 2], 16)

            for half, func in ((0, ACT.Copy), (1, ACT.Sigmoid)):
                with act.Fori(0, 2) as i:
                    for pr in range(2):
                        for j in range(CH):
                            vo_out(4 * half + 2 * i + pr, pr, 2 * half + i, func, j)
                            if half == 0 and j in (3, 7):
                                silu(4 * i + 2 * pr + j // 4, j // 4)

            def load_v(n):
                act.dma_start(vb[:, :, 0:HC], vod[n, :, 0:D].rearrange("p (h e) -> p h e", h=H)
                              if isinstance(n, int) else
                              vod[ds(n, 1), :, 0:D].rearrange("a p (h e) -> (a p) h e", h=H)).then_inc(v_in, 16)

            def load_o(n):
                act.dma_start(ob[:, :, :], vod[n, :, D:2 * D].rearrange("p (h e) -> p h e", h=H)
                              if isinstance(n, int) else
                              vod[ds(n, 1), :, D:2 * D].rearrange("a p (h e) -> (a p) h e", h=H)).then_inc(o_in, 16)

            def keys_queries(n):
                for w, (dst, sc, b0) in enumerate(((ck, HC ** -0.5, 2), (cq, 1.0, 6))):
                    act.wait_ge(qk_done, 2 * n + w + 1)
                    act.activation(dst[:, :, :].rearrange("p a t -> p (a t)"),
                                   ps[:, b0:b0 + 2, :].rearrange("p b t -> p (b t)"),
                                   ACT.Copy, scale=sc).then_inc(qk_out, 1)

            def powers(n):
                act.wait_ge(dwm_ready, n + 1)
                for h in range(H):
                    ins = act.activation(dw[:, h, :], dw[:, h, :], ACT.Exp,
                                         bias=cols[:, ds(n, 1), 0, h:h + 1].rearrange("p a h -> p (a h)"))
                ins.then_inc(dw_ready, 1)
                act.wait_ge(ktr_done, n + 1)
                for h in range(H):
                    act.activation(kw[:, 2 * h:2 * h + 2, :].rearrange("p a d -> p (a d)"),
                                   ps[:, h // 2, (h % 2) * HC:(h % 2) * HC + HC], ACT.Copy,
                                   scale=cols[:, ds(n, 1), 3, h:h + 1].rearrange("p a h -> p (a h)")).then_inc(kw_ready, 1)

            def out_high(n, col, width):
                act.wait_ge(htr_done, 1 + n + 1)
                for t in range(KT):
                    ins = act.activation(xh[:, t, ds(col, width)], ps[:, 6 + t // 4, (t % 4) * P:(t % 4) * P + width],
                                         ACT.Copy, scale=vec("c_g", t))
                ins.then_inc(ch_ready, 1)

            def chunk(n, last, nxt):
                act.wait_ge(cup_read, 1 + 8 * n)
                for h in range(H):
                    act.wait_ge(num_done, 4 * n + h + 1)
                    act.activation(iq[:, h, :], bank((7, 3)[h % 2], HC + 1), ACT.Copy,
                                   scale=cols[:, ds(n, 1), 1, h:h + 1].rearrange("p a h -> p (a h)")).then_inc(iq_ready, 1)
                if last is not None:
                    out_high(*last)
                if nxt is not None:
                    act.wait_ge(cup_done, 8 * n + 8)
                    load_v(nxt)
                    keys_queries(nxt)
                    act.wait_ge(cup_read, 1 + 8 * n + 8)
                    load_o(nxt)
                    powers(nxt)
                act.wait_ge(var_ready, 4 * n + 4)
                act.activation(st[:, 40:44], st[:, 25:32:2], ACT.Sqrt, bias=vec("eps")).then_inc(sd_ready, 1)

            for j in range(2):
                act.wait_ge(stage_out[j], 16 + 16 * CH * 4)
            act.wait_ge(c_zero, 2)
            load_v(0)
            load_o(0)
            act.wait_ge(acc_free, FREE0["vo1"] + 72)
            keys_queries(0)
            powers(0)
            chunk(0, None, 1)
            with act.Fori(1, CH - 2) as i:
                chunk(i, (i - 1, i * P - P, P), i + 1)
            chunk(CH - 2, (CH - 3, (CH - 3) * P, P), CH - 1)
            act.wait_ge(cup_read, 1 + 8 * (CH - 1))
            act.dma_start(O["c_o"][0], cs[:, :, :, :]).then_inc(c_sent, 16)
            act.wait_ge(c_sent, 16)
            act.dma_start(cs[:, :, :, :], I["c0"]).then_inc(c_swap, 16)
            chunk(CH - 1, (CH - 2, (CH - 2) * P, P), None)
            out_high(CH - 1, TP, TS)
            act.wait_ge(cup_read, 1 + 8 * CH)
            act.dma_start(O["c_o"][1], cs[:, :, :, :]).then_inc(c_sent, 16)
            act.wait_ge(qk_done, 2 * CH)
            act.dma_start(x[:, :, :], xsave).then_inc(x_in, 16)
            act.wait_ge(cl_ready, 1 + CH)
            act.wait_ge(c_sent, 32)
            act.dma_start(praw[:, :, :], I["pT"][1]).then_inc(p_in, 16)
            act.wait_ge(acc_free, FREE0["out1"] + 24)
            norm(3)
            ffn(1)
            ple(1, B1_PLE)
            act.wait_ge(ple_added, 1 + 48)
            norm(4)
            for tt in range(NT):
                act.wait_ge(xt_ready, 1 + KT * NT * 4 + KT * (tt + 1))
                sl = slice(tt * TW, (tt + 1) * TW)
                act.dma_start(O["yT"][:, :, sl], ybuf[:, :, sl]).then_inc(y_sent, 16)
            act.wait_ge(y_sent, 16 * NT)
            for s_, n_ in ((aconv_sent, 32), (kv_sent, 48), (ah_sent, 16), (cconv_sent, 32), (m_sent, 16)):
                act.wait_ge(s_, n_)


def tiles(v):
    return v.reshape(-1, P).T


def blocks(w):
    n = w.shape[1] // P
    return w.reshape(KT, P, n, P).transpose(2, 1, 0, 3).reshape(n, P, KT * P)


def pairs(w):
    return w.reshape(2, P, 2, 4, P).transpose(2, 1, 3, 0, 4).reshape(2, P, KT * P)


def block_diagonal(w):
    n, b, _ = w.shape
    per = P // b
    out = np.zeros((P, n // per, P), w.dtype)
    for i in range(n):
        t, r = i // per, (i % per) * b
        out[r:r + b, t, r:r + b] = w[i]
    return out


_OUT = {"yT": (P, KT, TOK), "a_conv_o": (P, AT, 6), "a_h_o": (P, 2, AT), "k_o": (P, P + TS), "v_o": (P, P + TS),
        "c_conv_o": (P, KT, 6), "c_o": (2, P, H, 2, HC + 1), "m_o": (H, 2)}


def kernel(x_prompt, x_sample, cache_a_conv, state_a_h, cache_b_k, cache_b_v, cache_c_conv, state_c_C, state_c_n,
           state_c_m, p_prompt, p_sample, norm_mix_g, norm_ffn_g, final_g, ab_w_in, ab_conv_w, ab_conv_b, ab_w_r,
           ab_b_r, ab_w_i, ab_b_i, ab_lambda, ab_sinks, ab_w_out, c_w_in, c_b_gate, c_conv_w, c_conv_b, c_w_q,
           c_w_k, c_norm_g, c_w_out, ffn_w_in, ffn_w_out, ple_w_proj, ple_w_gate):
    import concourse.bacc as bacc
    from concourse.bass_utils import run_bass_kernel_spmd

    f = np.float32
    a = {}

    def feature_major(prompt, sample):
        v = np.concatenate([prompt[0], sample[0]], axis=0)
        return v.T.reshape(-1, P, TOK).transpose(1, 0, 2)

    a["xT"] = feature_major(x_prompt, x_sample)
    a["pT"] = np.stack([feature_major(p_prompt[j], p_sample[j]) for j in range(2)])
    w = np.asarray(ab_w_in[0])
    g, u, q, k, v = np.split(w, [512, 1024, 1536, 1664], axis=1)
    q = q.reshape(D, 2, 4, HD).transpose(0, 2, 1, 3).reshape(D, 512)
    wo = np.asarray(ab_w_out[0])
    wo = np.concatenate([wo[:512], wo[512:].reshape(2, 4, HD, D).transpose(1, 0, 2, 3).reshape(512, D)])
    wc = np.asarray(c_w_in[0])
    gates = np.zeros((D, P), f)
    gates[:, 0:H] = wc[:, 3 * D:3 * D + H]
    gates[:, 32:32 + H] = wc[:, 3 * D + H:]

    def ffn(j):
        wi, wd = np.asarray(ffn_w_in[j]), np.asarray(ffn_w_out[j])
        gate, up = blocks(wi[:, :F_TILES * P]), blocks(wi[:, F_TILES * P:])
        ups = [np.stack([b for t in (2 * c, 2 * c + 1) for b in (gate[t], up[t])]) for c in range(FCH)]
        downs = [pairs(wd[256 * c:256 * (c + 1)]) for c in range(FCH)]
        out = [ups[0]]
        for c in range(FCH - 1):
            out += [ups[c + 1], downs[c]]
        return out + [downs[-1]]

    def ple(j):
        return [pairs(np.asarray(ple_w_proj[j])), blocks(np.asarray(ple_w_gate[j]))]

    a["wstream"] = np.concatenate(
        [blocks(np.concatenate([u, k, v, q, g], axis=1)), blocks(wo)] + ffn(0) + ple(0)
        + [blocks(gates), blocks(wc[:, :D]), np.zeros((1, P, D), f), blocks(wc[:, D:3 * D]),
           blocks(np.asarray(c_w_out[0]))] + ffn(1) + ple(1))
    assert a["wstream"].shape[0] == NBLK
    vecs = np.zeros((P, NVEC), f)

    def put(name, v):
        v = np.asarray(v)
        vecs[:, VEC[name]:VEC[name] + v.shape[1]] = v

    put("g_mix0", tiles(norm_mix_g[0]))
    put("g_ffn0", tiles(norm_ffn_g[0]))
    put("g_mix1", tiles(norm_mix_g[1]))
    put("g_ffn1", tiles(norm_ffn_g[1]))
    put("g_fin", tiles(final_g))
    put("a_w", np.concatenate([tiles(ab_conv_w[0, j]) for j in range(4)], axis=1))
    put("a_b", tiles(ab_conv_b[0]))
    put("b_r", tiles(ab_b_r[0]))
    put("b_i", tiles(ab_b_i[0]))
    put("lam", tiles(ab_lambda[0]))
    put("h0", tiles(state_a_h[0, 0]))
    put("sink", np.broadcast_to(ab_sinks[0], (P, 8)))
    put("c_w", np.concatenate([tiles(c_conv_w[0, j]) for j in range(4)], axis=1))
    put("c_b", tiles(c_conv_b[0]))
    put("c_g", tiles(c_norm_g[0]))
    vecs[0:H, VEC["b_gate"]] = c_b_gate[0, :H]
    vecs[32:32 + H, VEC["b_gate"]] = c_b_gate[0, H:]
    vecs[0:H, VEC["m0"]] = state_c_m[0, 0]
    vecs[:, VEC["eps"]] = EPS
    a["vecs"] = vecs
    a["ones"] = np.ones((P, P), f)
    a["ident"] = np.eye(P, dtype=f)
    a["lbd"] = np.stack([block_diagonal(np.asarray(ab_w_r[0])), block_diagonal(np.asarray(ab_w_i[0]))], axis=1)
    a["cbd"] = np.stack([block_diagonal(np.asarray(c_w_q[0])), block_diagonal(np.asarray(c_w_k[0]))], axis=1)
    a["a_conv"] = cache_a_conv[0, 0].reshape(3, AT, P).transpose(2, 1, 0)
    a["c_conv"] = cache_c_conv[0, 0].reshape(3, KT, P).transpose(2, 1, 0)
    a["kc"] = cache_b_k[0, 0].reshape(P, P).T
    a["vc"] = cache_b_v[0, 0].reshape(P, P)
    c0 = np.asarray(state_c_C[0, 0]).reshape(H, 2, P, HC).transpose(2, 0, 1, 3)
    n0 = np.asarray(state_c_n[0, 0]).reshape(H, 2, P).transpose(2, 0, 1)[..., None]
    a["c0"] = np.concatenate([c0, n0], axis=3)
    qi, kj = np.arange(P)[:, None], np.arange(2 * P)[None, :] - P
    back = qi // 64 - kj // 64
    seen = (back >= 0) & (back <= 2)
    d = np.abs(qi - kj).astype(f)
    far = f(1e30)
    a["dist"] = np.stack([np.where(seen & (kj >= 0), d, far), np.where(seen, d, far), np.where(kj < TS, d, far)],
                         axis=1).astype(f)
    a["sel"] = np.repeat(np.eye(H, dtype=f)[:, :, None], P, axis=2)
    a["cmask"] = np.where(np.arange(P)[:, None] <= np.arange(P)[None, :], f(0), f(NEG)).astype(f)

    nc = bacc.Bacc("TRN2", target_bir_lowering=False, num_devices=1)
    a = {n: np.ascontiguousarray(v, dtype=f) for n, v in a.items()}
    ins = {n: nc.dram_tensor(n, v.shape, F32, kind="ExternalInput").ap() for n, v in a.items()}
    outs = {n: nc.dram_tensor(n, s, F32, kind="ExternalOutput").ap() for n, s in _OUT.items()}
    build(nc, ins, outs)
    r = run_bass_kernel_spmd(nc, [a], core_ids=[0]).results[0]

    y = r["yT"].transpose(1, 0, 2).reshape(D, TOK).T
    a_conv, c_conv = (r[n].transpose(2, 1, 0).reshape(2, 3, -1) for n in ("a_conv_o", "c_conv_o"))
    a_h = r["a_h_o"].transpose(1, 2, 0).reshape(2, -1)
    kk, vv = r["k_o"].T, r["v_o"].T
    c = r["c_o"].transpose(0, 2, 3, 1, 4)
    m = r["m_o"].T
    cc = [c[j, ..., :HC].reshape(1, 1, H, HC, HC) for j in range(2)]
    cn = [c[j, ..., HC].reshape(1, 1, H, HC) for j in range(2)]
    out = []
    for j in range(2):
        rows_ = slice(0, P) if j == 0 else slice(P, P + TS)
        out.append([a_conv[j][None, None], a_h[j][None, None], kk[rows_].reshape(1, 1, -1, 2, HD),
                    vv[rows_].reshape(1, 1, -1, 2, HD), c_conv[j][None, None], cc[j], cn[j], m[j].reshape(1, 1, H)])
    return tuple([y[:TP][None], y[TP:][None]] + out[0] + out[1])
```

```python
from contextlib import ExitStack, contextmanager

import numpy as np
import concourse.bass as bass
from concourse import mybir

F32 = mybir.dt.float32
F32R = mybir.dt.float32r
ALU = mybir.AluOpType
ACT = mybir.ActivationFunctionType
AX = mybir.AxisListType
ds = bass.ds

P = 128
D = 1024
KT = D // P
TP, TS = 1024, 32
TOK = TP + TS
NT = 3
TW = TOK // NT
LAST = TP - 2 * TW
EPS = 1e-6
NEG = -1e30
AT = 4
UA = 3 + TP + 3 + TS
CA = UA - 3
SA = TP + 3
HD = 64
SLOTS = 11
NQ = 9
CH = 9
H = 4
HC = 256
UC = 3 + TP + 3 + P
CC = UC - 3
F_TILES = 22
FCH = F_TILES // 2
SLOPE = [2.0 ** -(h + 1) for h in range(8)]

B_IN0, B_OUT0, B_FFN, B_PLE = 14, 8, 6 * FCH, 10
B0_IN = 0
B0_OUT = B0_IN + B_IN0
B0_FFN = B0_OUT + B_OUT0
B0_PLE = B0_FFN + B_FFN
B1_GATE = B0_PLE + B_PLE
B1_U = B1_GATE + 1
B1_PAD = B1_U + 8
B1_VO = B1_PAD + 1
B1_OUT = B1_VO + 16
B1_FFN = B1_OUT + 8
B1_PLE = B1_FFN + B_FFN
NBLK = B1_PLE + B_PLE
NW = 4
NRAW = 2

VEC = {}
_at = 0
for _n, _w in (("g_mix0", 8), ("g_ffn0", 8), ("g_mix1", 8), ("g_ffn1", 8), ("g_fin", 8),
               ("a_w", 16), ("a_b", 4), ("b_r", 4), ("b_i", 4), ("lam", 4), ("h0", 4),
               ("sink", 8), ("c_w", 32), ("c_b", 8), ("c_g", 8), ("b_gate", 1), ("m0", 1), ("eps", 1)):
    VEC[_n] = _at
    _at += _w
NVEC = (_at + 7) // 8 * 8
assert B1_VO % NW in (0, 2)


class Steps:

    def __init__(self, eng, sem):
        self.eng, self.sem, self.base, self.n = eng, sem, 0, 0

    def mark(self, ins):
        ins.then_inc(self.sem, 1)
        self.n += 1

    def wait(self):
        self.eng.wait_ge(self.sem, self.base + self.n)

    def __call__(self, ins):
        self.mark(ins)
        self.wait()

    @contextmanager
    def loop(self, first, end, marks):
        base, n = self.base, self.n
        with self.eng.Fori(first, end) as i:
            self.base, self.n = base + n + (i - first) * marks, 0
            yield i
            assert self.n == marks, (self.n, marks)
        self.base, self.n = base + n + (end - first) * marks, 0


def build(nc, I, O):
    with ExitStack() as ctx:
        base = (nc.sbuf_base + 31) // 32 * 32

        def at(name, off, shape, dt=F32):
            return nc.alloc_sbuf_tensor_at(name, shape, dt, offset=base + 4 * off, align_bytes=4)

        def sem(name):
            return ctx.enter_context(nc.semaphore(name))

        o_wh = NRAW * 1024
        o_wl = o_wh + NW * 1024
        o_xh = o_wl + NW * 1024
        XP = KT * TOK + 96
        o_xl = o_xh + XP
        o_x = o_xl + XP
        m = o_x + KT * TOK
        raw = at("raw", 0, [P, NRAW, KT * P])
        wh = at("wh", o_wh, [P, NW, KT, P], F32R)
        wl = at("wl", o_wl, [P, NW, KT, P], F32R)
        xh_flat = at("xh", o_xh, [P, XP], F32R)
        xl_flat = at("xl", o_xl, [P, XP], F32R)
        xh = xh_flat[:, 0:KT * TOK].rearrange("p (k t) -> p k t", k=KT)
        xl = xl_flat[:, 0:KT * TOK].rearrange("p (k t) -> p k t", k=KT)
        x = at("x", o_x, [P, KT, TOK])
        hh = at("hh", m, [P, 2, 2, TOK], F32R)
        hl = at("hl", m + 4224, [P, 2, 2, TOK], F32R)
        pp = at("pp", m, [P, KT, TOK])
        ph = at("ph", m + 8448, [P, 2, TOK], F32R)
        pl = at("pl", m + 10560, [P, 2, TOK], F32R)
        praw = at("praw", m + 12672, [P, 2, TOK])
        ybuf = at("ybuf", m, [P, KT, TOK])
        tmpa = at("tmpa", m + 14784, [P, 2, TW])
        tmpb = at("tmpb", m + 15488, [P, 2, TW])
        tmp = at("tmp", m + 14784, [P, 4, TW])
        sqsum = at("sqsum", m + 11504, [P, TOK])
        rt = at("rt", m + 16192, [P, TW])
        rstd = at("rstd", m + 16544, [P, TW])
        vecs = at("vecs", m + 16896, [P, NVEC])
        ones = at("ones", m + 16896 + NVEC, [P, P])
        ident = at("ident", m + 16896 + NVEC + 128, [P, P])
        asmall = at("asmall", m + 16896 + NVEC + 256, [P, 8, AT])
        seeds = at("seeds", m + 16896 + NVEC + 288, [P, 24])
        assert NVEC + 256 + 32 + 24 <= 544
        sqx = at("sqx", m + 4248, [P, 12, TW])
        ua = at("ua", m, [P, AT, UA])
        uc = [at("uc0", m + 4248, [P, CA]), at("uc1", m + 14784, [P, CA])]
        lr1 = at("lr1", m + 4248 + CA, [P, CA])
        lr2 = at("lr2", m + 4248 + 2 * CA, [P, CA])
        lr3 = at("lr3", m + 4248 + 3 * CA, [P, CA])
        lbd = at("lbd", m + 8484, [P, 2, AT, P])
        dist = at("dist", m + 9508, [P, 3, 2 * P])
        kt = at("kt", m + 10788, [P, SLOTS * P])
        vtok = at("vtok", m + 12196, [P, SLOTS, P])
        vt = at("vt", m + 13604, [P, TOK])
        lr4 = at("lr4", m + 13604, [P, CA])
        ss = at("ss", m, [P, 2, 4, 2 * P])
        pts = at("pts", m + 2048, [P, 8, P])
        otok = at("otok", m + 3072, [P, 4, 2, HD])
        qs = at("qs", m + 3584, [P, 4, P])
        ks = at("ks", m + 4096, [P, 2 * P])
        sm = at("sm", m + 4352, [P, 2, 6, 4])
        ga = at("ga", o_x, [P, 4, TOK])
        qt0 = at("qt0", o_x + 4 * TOK, [P, 4, TOK])
        uu = at("uu", o_x, [P, KT, UC])
        c = o_x + KT * UC
        cbd = at("cbd", c, [P, 2, KT, P])
        sel = at("sel", c + 2048, [4, 4, P])
        arow = at("arow", c + 2560, [4, CH * P])
        cols = at("cols", c + 3712, [P, CH, 4, H])
        decay = at("decay", c + 3856, [P, CH, H])
        cmask = at("cmask", c + 3892, [P, P])
        stage = at("stage", c + 4020, [P, 2, 2 * P])
        cq = at("cq", c + 4532, [P, KT, P])
        ck = at("ck", c + 5556, [P, KT, P])
        vb = at("vb", c + 6580, [P, H, HC + 1])
        ob = at("ob", c + 7608, [P, H, HC])
        cs = at("cs", c + 8632, [P, H, 2, HC + 1])
        kw = at("kw", c + 10688, [P, KT, P])
        dw = at("dw", c + 11712, [P, H, P])
        sw = at("sw", c + 12224, [P, H, P])
        hb = at("hb", c + 12736, [P, H, HC])
        rows = at("rows", c + 6580, [4, 6, CH * P])
        ct = [at("ct0", c + 4532, [P, CC]), at("ct1", c + 10688, [P, CC])]
        assert c + 13760 <= m + 14784
        iq = at("iq", m + 14784, [P, H, HC + 1])
        st = at("st", m + 15812, [P, 128])
        rsmall = at("rsmall", m + 15812 + 128, [4, 64])

        ps = ctx.enter_context(nc.psum_tensor("ps", [P, 8, 512], F32))

        def bank(b, n=TW):
            return ps[:, b, 0:n]

        xsave = nc.dram_tensor("xsave", [P, KT, TOK], F32, kind="Internal").ap()
        vod = nc.dram_tensor("vod", [CH, P, 2 * D], F32, kind="Internal").ap()

        raw_landed = [sem(f"raw_landed{i}") for i in range(NRAW)]
        raw_free = sem("raw_free")
        hi_made = sem("hi_made")
        zero_ready = sem("zero_ready")
        block_done = sem("block_done")
        acc_done = sem("acc_done")
        acc_free = sem("acc_free")
        init_done = sem("init_done")
        const_in = sem("const_in")
        m0_in = sem("m0_in")
        lam_abs = sem("lam_abs")
        lam_exp = sem("lam_exp")
        sp_ready = sem("sp_ready")
        aconv_sent = sem("aconv_sent")
        kv_sent = sem("kv_sent")
        ah_kept = sem("ah_kept")
        ah_sent = sem("ah_sent")
        cconv_sent = sem("cconv_sent")
        m_kept = sem("m_kept")
        m_sent = sem("m_sent")
        c_sent = sem("c_sent")
        y_sent = sem("y_sent")
        x_in = sem("x_in")
        xt_in = [sem(f"xt_in{i}") for i in range(NT)]
        sq_ready = sem("sq_ready")
        sq_added = sem("sq_added")
        ss_done = sem("ss_done")
        rt_ready = sem("rt_ready")
        rstd_ready = sem("rstd_ready")
        xt_ready = sem("xt_ready")
        xh_ready = sem("xh_ready")
        xl_ready = sem("xl_ready")
        dve_step = sem("dve_step")
        uc_ready = sem("uc_ready")
        gate_done = sem("gate_done")
        gate_out = sem("gate_out")
        et_ready = sem("et_ready")
        iu_done = sem("iu_done")
        sq4_ready = sem("sq4_ready")
        h_ready = sem("h_ready")
        vtr_done = sem("vtr_done")
        v_ready = sem("v_ready")
        y_ready = sem("y_ready")
        yh_ready = sem("yh_ready")
        yl_ready = sem("yl_ready")
        qk_staged = sem("qk_staged")
        s_done = sem("s_done")
        s_read = sem("s_read")
        nm_ready = sem("nm_ready")
        exp_done = sem("exp_done")
        pt_done = sem("pt_done")
        pt_out = sem("pt_out")
        o_done = sem("o_done")
        o_read = sem("o_read")
        ot_done = sem("ot_done")
        oh_ready = sem("oh_ready")
        ol_ready = sem("ol_ready")
        pair_done = sem("pair_done")
        sil_ready = sem("sil_ready")
        h32_ready = sem("h32_ready")
        hh_ready = sem("hh_ready")
        hl_ready = sem("hl_ready")
        down_done = sem("down_done")
        down_added = sem("down_added")
        p_in = sem("p_in")
        ph_ready = sem("ph_ready")
        pl_ready = sem("pl_ready")
        sg_ready = sem("sg_ready")
        ple_added = sem("ple_added")
        x_saved = sem("x_saved")
        c_in = sem("c_in")
        fabs_ready = sem("fabs_ready")
        fexp_ready = sem("fexp_ready")
        rows_log = sem("rows_log")
        rows_ready = sem("rows_ready")
        pads_ready = sem("pads_ready")
        cols_done = sem("cols_done")
        cols_out = sem("cols_out")
        ct_ready = sem("ct_ready")
        silu_done = sem("silu_done")
        stage_out = [sem("stage_out0"), sem("stage_out1")]
        v_in = sem("v_in")
        o_in = sem("o_in")
        qk_done = sem("qk_done")
        qk_out = sem("qk_out")
        ab_done = sem("ab_done")
        dwm_ready = sem("dwm_ready")
        dw_ready = sem("dw_ready")
        st_done = sem("st_done")
        sw_ready = sem("sw_ready")
        ktr_done = sem("ktr_done")
        kw_ready = sem("kw_ready")
        num_done = sem("num_done")
        iq_ready = sem("iq_ready")
        num_read = sem("num_read")
        cup_done = sem("cup_done")
        cup_read = sem("cup_read")
        var_ready = sem("var_ready")
        sd_ready = sem("sd_ready")
        hb_ready = sem("hb_ready")
        htr_done = sem("htr_done")
        ch_ready = sem("ch_ready")
        cl_ready = sem("cl_ready")
        c_zero = sem("c_zero")
        c_swap = sem("c_swap")
        block = ctx.enter_context(nc.Block())

        def vec(name, j=0, n=1):
            return vecs[:, VEC[name] + j:VEC[name] + j + n]

        phases = (("in0", 14, 3 * 14), ("out0", 8, 24), ("proj0", 2, 24), ("gate0", 8, 24),
                  ("g1", 1, 3), ("u1", 8, 24), ("vo1", 16, 72), ("out1", 8, 24),
                  ("proj1", 2, 24), ("gate1", 8, 24))
        DONE0, FREE0, OFF = {}, {}, {}
        nd, nf = 0, 6
        for name, nb, units in phases:
            DONE0[name], FREE0[name], OFF[name] = nd, nf, nf % 6
            ends = {"proj0": 1, "proj1": 1, "vo1": 8}.get(name, nb)
            nd += units - ends
            nf += units
        XLN = {n: KT * NT * j for j, n in enumerate(("mix0", "ffn0", "ple0", "mix1", "ffn1", "ple1"))}
        DA = 24

        def hilo(pe, out, whi, wlo, mhi, mlo, first, last):
            pe.matmul(out, whi, mhi, start=first, stop=False)
            pe.matmul(out, whi, mlo, start=False, stop=False)
            return pe.matmul(out, wlo, mhi, start=False, stop=last)

        @block.sync
        def _(sp):
            with sp.Fori(0, NBLK // NRAW) as i:
                for j in range(NRAW):
                    sp.wait_ge(raw_free, NRAW * i + j + 1)
                    sp.dma_start(raw[:, j, :], I["wstream"][NRAW * i + j]).then_inc(raw_landed[j], 16)

        @block.gpsimd
        def _(pool):
            pool.memset(seeds[:, 0:1], 0.0).then_inc(raw_free, NRAW)
            pool.memset(seeds[:, 1:2], 0.0).then_inc(block_done, NW)
            pool.memset(seeds[:, 2:3], 0.0).then_inc(acc_free, 6)
            pool.memset(seeds[:, 3:4], 0.0).then_inc(down_added, DA)
            pool.memset(seeds[:, 4:5], 0.0).then_inc(silu_done, 2)
            for j, s_ in enumerate((rt_ready, rstd_ready, ss_done, xt_ready, xl_ready, cl_ready, num_read, cup_read,
                                    hb_ready, htr_done, ple_added)):
                pool.memset(seeds[:, 8 + j:9 + j], 0.0).then_inc(s_, 1)
            for j in range(2):
                pool.memset(seeds[:, 20 + j:21 + j], 0.0).then_inc(stage_out[j], 16)
            pool.memset(seeds[:, 6:7], 0.0).then_inc(zero_ready, 1)
            zero = seeds[:, 6:7].to_broadcast([P, KT * P])
            pool.wait_ge(zero_ready, 1)
            with pool.Fori(0, NBLK // NW) as i:
                for j in range(NW):
                    r = j % NRAW
                    pool.wait_ge(raw_landed[r], 16 * (NW // NRAW) * i + 16 * (j // NRAW + 1))
                    pool.wait_ge(block_done, NW * i + j + 1)
                    hi = wh[:, j, :, :].rearrange("p k c -> p (k c)")
                    lo = wl[:, j, :, :].rearrange("p k c -> p (k c)")
                    pool.tensor_tensor(hi, raw[:, r, :], zero, ALU.add).then_inc(hi_made, 1)
                    pool.wait_ge(hi_made, NW * i + j + 1)
                    pool.tensor_tensor(lo, raw[:, r, :], hi.bitcast(F32), ALU.subtract).then_inc(raw_free, 1)

        def split_count(b):
            return b + 1 + NRAW

        def done_count(b):
            return b + 1 + NW

        @block.tensor
        def _(pe):
            def input_sums():
                for tt in range(NT):
                    if tt == 2:
                        pe.wait_ge(rt_ready, 2)
                    for k in range(KT):
                        pe.wait_ge(sq_ready, KT * tt + k + 1)
                        mm = pe.matmul(bank(6 + tt % 2), ones[:, :], sqx[:, (KT * tt + k) % 12, :],
                                       start=(k == 0), stop=(k == KT - 1))
                    mm.then_inc(ss_done, 1)

            def norm(ni):
                for tt in range(NT):
                    pe.wait_ge(sq_added, 25 * ni - 3 + tt + 1)
                    pe.wait_ge(rt_ready, 1 + 3 * ni + tt // 2)
                    pe.matmul(bank(6 + tt % 2), ones[:, :], sqsum[:, tt * TW:(tt + 1) * TW],
                              start=True, stop=True).then_inc(ss_done, 1)

            def dense(slot, b, free, bank0, xl_at=None):
                pe.wait_ge(raw_free, split_count(b))
                for tt in range(NT):
                    pe.wait_ge(acc_free, free + tt + 1)
                    for k in range(KT):
                        if xl_at is not None:
                            pe.wait_ge(xl_ready, 1 + xl_at + KT * tt + k + 1)
                        mm = hilo(pe, bank(bank0 + tt), wh[:, slot, k, :], wl[:, slot, k, :],
                                  xh[:, k, tt * TW:(tt + 1) * TW], xl[:, k, tt * TW:(tt + 1) * TW],
                                  k == 0, k == KT - 1)
                    mm.then_inc(acc_done if tt < NT - 1 else block_done, 1)

            def dense_loop(phase, b0, nb, xl_at=None):
                with pe.Fori(0, nb // NW) as i:
                    for j in range(NW):
                        dense((b0 + j) % NW, b0 + NW * i + j, FREE0[phase] - 6 + (NW * i + j) * 3,
                              (OFF[phase] + 3 * j) % 6, xl_at if j == 0 else None)

            def lru_gates(t):
                pe.wait_ge(uc_ready, t + 1)
                for u in range(6):
                    w, tt = u // 3, u % 3
                    n = 6 * t + u
                    if n >= 2:
                        pe.wait_ge(gate_out, n - 1)
                    pe.matmul(bank(6 + u % 2, 353), lbd[:, w, t, :], uc[t % 2][:, tt * 353:(tt + 1) * 353],
                              start=True, stop=True).then_inc(gate_done, 1)

            def scores(n, kvh):
                pe.wait_ge(qk_staged, 2 * n + 2)
                if not (isinstance(n, int) and n == 0):
                    pe.wait_ge(s_read, 2 * n + kvh - 1)
                for g in range(4):
                    out = ps[:, 2 * kvh + g // 2, (g % 2) * 256:(g % 2) * 256 + 256]
                    mm = pe.matmul(out, qs[kvh * HD:(kvh + 1) * HD, g, :], ks[kvh * HD:(kvh + 1) * HD, :],
                                   start=True, stop=True)
                mm.then_inc(s_done, 1)

            def transpose_p(n, kvh):
                pe.wait_ge(exp_done, 2 * n + kvh + 1)
                if not (isinstance(n, int) and n == 0 and kvh == 0):
                    pe.wait_ge(pt_out, 2 * n + kvh)
                for g in range(4):
                    for kk in range(2):
                        j = 2 * g + kk
                        mm = pe.transpose(ps[:, 4 + j // 4, (j % 4) * P:(j % 4 + 1) * P],
                                          ss[:, kvh, g, kk * P:(kk + 1) * P], ident[:, :])
                mm.then_inc(pt_done, 1)

            def outputs(n, kvh, vslot):
                pe.wait_ge(pt_out, 2 * n + kvh + 1)
                if not (isinstance(n, int) and n == 0 and kvh == 0):
                    pe.wait_ge(o_read, 2 * n + kvh)
                for g in range(4):
                    for kk in range(2):
                        mm = pe.matmul(ps[:, 6, (2 * g + kvh) * HD:(2 * g + kvh + 1) * HD],
                                       pts[:, 2 * g + kk, :], vtok[:, vslot + kk, kvh * HD:(kvh + 1) * HD],
                                       start=(kk == 0), stop=(kk == 1))
                mm.then_inc(o_done, 1)

            def transpose_o(n):
                pe.wait_ge(o_read, 2 * n + 2)
                for g in range(4):
                    mm = pe.transpose(ps[:, 7, g * P:(g + 1) * P],
                                      otok[:, g, :, :].rearrange("p a d -> p (a d)"), ident[:, :])
                mm.then_inc(ot_done, 1)

            def attend(n, vslot, more=True):
                if more:
                    scores(n + 1, 0)
                if not (isinstance(n, int) and n == 0):
                    outputs(n - 1, 1, n - 1)
                transpose_p(n, 0)
                if more:
                    scores(n + 1, 1)
                if not (isinstance(n, int) and n == 0):
                    transpose_o(n - 1)
                outputs(n, 0, vslot)
                transpose_p(n, 1)

            def ffn(layer, b0):
                xl_at = XLN[f"ffn{layer}"]
                c0 = FCH * layer

                def up(cx, b, slot0, first=False):
                    for f in range(2):
                        pe.wait_ge(raw_free, split_count(b + 2 * f + 1))
                        for tt in range(NT):
                            pair = 6 * cx + 3 * f + tt
                            if not (first and f == 0):
                                pe.wait_ge(h32_ready, pair - 2)
                            if not first and f == 0:
                                pe.wait_ge(down_added, DA + 24 * (cx - 2) + 18 + 2 * tt)
                            for w in range(2):
                                slot = (slot0 + 2 * f + w) % NW
                                for k in range(KT):
                                    if first and f == 0 and w == 0:
                                        pe.wait_ge(xl_ready, 1 + xl_at + KT * tt + k + 1)
                                    mm = hilo(pe, bank(2 * tt + w), wh[:, slot, k, :], wl[:, slot, k, :],
                                              xh[:, k, tt * TW:(tt + 1) * TW], xl[:, k, tt * TW:(tt + 1) * TW],
                                              k == 0, k == KT - 1)
                            if tt < 2:
                                mm.then_inc(pair_done, 1)
                            else:
                                mm.then_inc(block_done, 2)

                def down(cx, b, slot0, par, pairs):
                    pe.wait_ge(hl_ready, 6 * (cx + 1))
                    for u in range(24):
                        mo, tt = u // 3, u % 3
                        if u % 12 == 0:
                            pe.wait_ge(raw_free, split_count(b + u // 12))
                        if u < 6:
                            pe.wait_ge(h32_ready, pairs + u // 2 + 1)
                        pe.wait_ge(down_added, DA + 24 * cx + u - 7)
                        slot = (slot0 + u // 12) % NW
                        for kk in range(2):
                            wk = (mo % 4) * 2 + kk
                            mm = hilo(pe, bank(u % 8), wh[:, slot, wk, :], wl[:, slot, wk, :],
                                      hh[:, par, kk, tt * TW:(tt + 1) * TW], hl[:, par, kk, tt * TW:(tt + 1) * TW],
                                      kk == 0, kk == 1)
                        mm.then_inc(block_done if u % 12 == 11 else down_done, 1)

                up(c0, b0, b0 % NW, True)
                with pe.Fori(0, FCH // 2) as i:
                    for j in range(2):
                        cx = c0 + 2 * i + j
                        b = b0 + 4 + 6 * j + 12 * i
                        slot = (b0 + 4 + 6 * j) % NW
                        up(cx + 1, b, slot)
                        down(cx, b + 4, slot, j, 6 * (cx + 1) + 3)
                cx = c0 + FCH - 1
                down(cx, b0 + B_FFN - 2, (b0 + B_FFN - 2) % NW, (FCH - 1) % 2, 6 * cx + 3)

            def ple(layer, b0):
                pe.wait_ge(pl_ready, 2 * (layer + 1))
                pe.wait_ge(raw_free, split_count(b0 + 1))
                pe.wait_ge(down_added, DA + 24 * FCH * (layer + 1))
                for tt in range(NT):
                    for mo in range(KT):
                        u = KT * tt + mo
                        pe.wait_ge(acc_free, FREE0[f"proj{layer}"] - 6 + u + 1)
                        slot = (b0 + mo // 4) % NW
                        for kk in range(2):
                            wk = (mo % 4) * 2 + kk
                            mm = hilo(pe, bank((u + OFF[f"proj{layer}"]) % 6), wh[:, slot, wk, :], wl[:, slot, wk, :],
                                      ph[:, kk, tt * TW:(tt + 1) * TW], pl[:, kk, tt * TW:(tt + 1) * TW],
                                      kk == 0, kk == 1)
                        if u < 23:
                            mm.then_inc(acc_done, 1)
                        else:
                            mm.then_inc(block_done, 2)
                dense_loop(f"gate{layer}", b0 + 2, KT, XLN[f"ple{layer}"])

            pe.wait_ge(const_in, 16 * 3)
            input_sums()
            dense_loop("in0", B0_IN, 8, XLN["mix0"])
            pe.wait_ge(m0_in, 16 * 5)
            for j in range(9):
                n = P if j < 8 else TS
                if j == 0:
                    pe.wait_ge(acc_free, FREE0["in0"] + 3 * 6)
                if j == 4:
                    pe.wait_ge(v_ready, 1)
                if j == 8:
                    pe.wait_ge(v_ready, 2)
                mm = pe.transpose(ps[0:n, 7, (j % 4) * P:(j % 4 + 1) * P], vt[:, j * P:j * P + n], ident[:, :])
                if j in (3, 7, 8):
                    mm.then_inc(vtr_done, 1)
            pe.wait_ge(v_ready, 3)
            for j in range(8, 14):
                dense((B0_IN + j) % NW, B0_IN + j, FREE0["in0"] - 6 + 3 * j, (OFF["in0"] + 3 * j) % 6)
                if 8 <= j < 12:
                    lru_gates(j - 8)
            pe.wait_ge(acc_free, FREE0["in0"] + 42)
            pe.wait_ge(gate_out, 24)
            scores(0, 0)
            scores(0, 1)
            attend(0, 0)
            with pe.Fori(1, NQ - 3) as i:
                attend(i, i)
            attend(NQ - 3, NQ - 3)
            attend(NQ - 2, NQ - 2)
            attend(NQ - 1, NQ, False)
            outputs(NQ - 1, 1, NQ)
            transpose_o(NQ - 1)
            pe.wait_ge(yl_ready, AT)
            pe.wait_ge(ol_ready, NQ)
            dense_loop("out0", B0_OUT, KT)
            norm(1)
            ffn(0, B0_FFN)
            ple(0, B0_PLE)
            norm(2)
            dense(B1_GATE % NW, B1_GATE, FREE0["g1"] - 6, OFF["g1"], XLN["mix1"])
            dense_loop("u1", B1_U, KT)
            pe.wait_ge(rows_ready, 1)
            pe.wait_ge(c_in, 16 * 4)
            for cc in range(CH):
                for q in range(4):
                    r = (0, 5, 4, 1)[q]
                    pe.transpose(ps[:, 6, (cc * 4 + q) * 4:(cc * 4 + q + 1) * 4],
                                 rows[:, r, cc * P:(cc + 1) * P], ident[0:4, 0:4])
            for h in range(H):
                mm = pe.matmul(ps[:, 6, 256 + CH * h:256 + CH * (h + 1)], sel[:, h, :], rsmall[:, 32:32 + CH],
                               start=True, stop=True)
            mm.then_inc(cols_done, 1)
            for half in range(2):
                with pe.Fori(0, 2) as i:
                    for pr in range(2):
                        slot = (2 * pr + B1_VO) % NW
                        pair = 4 * half + 2 * i + pr
                        b = B1_VO + 2 * pair
                        pe.wait_ge(raw_free, split_count(b + 1))
                        for j in range(CH):
                            u = CH * pr + j
                            pe.wait_ge(acc_free, FREE0["vo1"] - 6 + 9 * pair + j + 1)
                            for k in range(KT):
                                mh = xh_flat[:, k * TOK + j * P:k * TOK + (j + 1) * P]
                                ml = xl_flat[:, k * TOK + j * P:k * TOK + (j + 1) * P]
                                out = ps[:, (u + OFF["vo1"]) % 6, 0:2 * P]
                                mm = hilo(pe, out, mh, ml, wh[:, slot:slot + 2, k, :], wl[:, slot:slot + 2, k, :],
                                          k == 0, k == KT - 1)
                            if j < CH - 1:
                                mm.then_inc(acc_done, 1)
                            else:
                                mm.then_inc(block_done, 2)

            def front(n, ucol):
                pe.wait_ge(num_read, 1 + 4 * n)
                for w, b0 in ((1, 2), (0, 6)):
                    if w == 0 and not (isinstance(n, int) and n == 0):
                        pe.wait_ge(cl_ready, n)
                    for t in range(KT):
                        mm = pe.matmul(ps[:, b0 + t // 4, (t % 4) * P:(t % 4 + 1) * P], cbd[:, w, t, :],
                                       uu[:, t, ds(ucol, P)], start=True, stop=True)
                    mm.then_inc(qk_done, 1)
                pe.wait_ge(cup_read, 1 + 8 * n)
                for h in range(H):
                    mm = pe.matmul(ps[:, 4, h * P:(h + 1) * P], sel[:, h, :], arow[:, ds(n * P, P)],
                                   start=True, stop=True)
                mm.then_inc(ab_done, 1)
                pe.wait_ge(qk_out, 2 * n + 1)
                for t in range(KT):
                    mm = pe.transpose(ps[:, t // 4, (t % 4) * P:(t % 4 + 1) * P], ck[:, t, :], ident[:, :])
                mm.then_inc(ktr_done, 1)
                pe.wait_ge(qk_out, 2 * n + 2)
                for h in range(H):
                    for dk in range(2):
                        mm = pe.matmul(ps[:, 5, h * P:(h + 1) * P], ck[:, 2 * h + dk, :], cq[:, 2 * h + dk, :],
                                       start=(dk == 0), stop=(dk == 1))
                mm.then_inc(st_done, 1)

            def transpose_h(n):
                pe.wait_ge(hb_ready, 1 + 4 * n + 4)
                for t in range(KT):
                    mm = pe.transpose(ps[:, 6 + t // 4, (t % 4) * P:(t % 4 + 1) * P],
                                      hb[:, t // 2, (t % 2) * P:(t % 2 + 1) * P], ident[:, :])
                mm.then_inc(htr_done, 1)

            def chunk(n, last):
                pe.wait_ge(v_in, 16 * (n + 1))
                pe.wait_ge(sw_ready, n + 1)
                for h in range(H):
                    if h >= 2:
                        pe.wait_ge(num_read, 1 + 4 * n + h - 1)
                    b0 = (6, 2)[h % 2]
                    for dk in range(2):
                        pe.matmul(bank(b0 + 1, HC + 1), cq[:, 2 * h + dk, :], cs[:, h, dk, :],
                                  start=(dk == 0), stop=(dk == 1))
                    pe.matmul(bank(b0, HC + 1), sw[:, h, :], vb[:, h, :], start=True, stop=True).then_inc(num_done, 1)
                pe.wait_ge(kw_ready, 4 * n + 4)
                for u in range(8):
                    if u == 2 and last is not None:
                        pe.wait_ge(num_read, 1 + 4 * n + 3)
                        transpose_h(last)
                    if u >= 4:
                        pe.wait_ge(cup_read, 1 + 8 * n + u - 3)
                    pe.matmul(bank((0, 1, 4, 5)[u % 4], HC + 1), kw[:, u, :], vb[:, u // 2, :],
                              start=True, stop=True).then_inc(cup_done, 1)

            pe.wait_ge(acc_free, FREE0["vo1"] + 72)
            pe.wait_ge(silu_done, KT + 2)
            pe.wait_ge(cols_out, 2)
            pe.wait_ge(c_zero, 2)
            front(0, 0)
            chunk(0, None)
            front(1, P)
            with pe.Fori(1, CH - 2) as i:
                chunk(i, i - 1)
                front(i + 1, i * P + P)
            chunk(CH - 2, CH - 3)
            front(CH - 1, TP + 3)
            pe.wait_ge(c_swap, 16)
            chunk(CH - 1, CH - 2)
            pe.wait_ge(num_read, 1 + 4 * CH)
            pe.wait_ge(cl_ready, CH)
            transpose_h(CH - 1)
            pe.wait_ge(cl_ready, 1 + CH)
            dense_loop("out1", B1_OUT, KT)
            norm(3)
            ffn(1, B1_FFN)
            ple(1, B1_PLE)
            norm(4)

        @block.vector
        def _(dve):
            step = Steps(dve, dve_step)

            def rstd_of(ni, tt):
                g = 3 * ni + tt
                dve.wait_ge(rt_ready, 1 + g + 1)
                dve.wait_ge(xt_ready, 1 + KT * g)
                dve.reciprocal(rstd[:, :], rt[:, :]).then_inc(rstd_ready, 1)

            def norm(ni):
                gname = ("g_mix0", "g_ffn0", "g_mix1", "g_ffn1")[ni]
                base_h = XLN[("mix0", "ffn0", "mix1", "ffn1")[ni]]

                def low(tt, k):
                    sl = slice(tt * TW, (tt + 1) * TW)
                    dve.wait_ge(xh_ready, base_h + KT * tt + k + 1)
                    dve.tensor_tensor(xl[:, k, sl], tmp[:, k % 4, :], xh[:, k, sl].bitcast(F32),
                                      ALU.subtract).then_inc(xl_ready, 1)

                rstd_of(ni, 0)
                for tt in range(NT):
                    dve.wait_ge(rstd_ready, 1 + 3 * ni + tt + 1)
                    for k in range(KT):
                        dve.wait_ge(xl_ready, 1 + base_h + max(KT * tt + k - 3, 0))
                        dve.scalar_tensor_tensor(tmp[:, k % 4, :], x[:, k, tt * TW:(tt + 1) * TW], vec(gname, k),
                                                 rstd[:, :], ALU.mult, ALU.mult).then_inc(xt_ready, 1)
                        if k >= 2:
                            low(tt, k - 2)
                    low(tt, KT - 2)
                    if tt < NT - 1:
                        rstd_of(ni, tt + 1)
                    low(tt, KT - 1)

            def clear_sums(ni):
                dve.memset(sqsum[:, :], 0.0).then_inc(sq_added, 1)

            def add_squares(ni, n, tt, xs, part):
                step(dve.tensor_tensor(tmpb[:, part, :], xs, xs, ALU.mult))
                dve.wait_ge(sq_added, 25 * (ni - 1) + 1 + 3 * n + tt)
                sl = slice(tt * TW, (tt + 1) * TW)
                dve.tensor_tensor(sqsum[:, sl], tmpb[:, part, :], sqsum[:, sl], ALU.add).then_inc(sq_added, 1)

            def unit_wait(tt, done, b):
                if tt < NT - 1:
                    dve.wait_ge(acc_done, done)
                else:
                    dve.wait_ge(block_done, done_count(b))

            def add_loop(phase, b0, ni):
                clear_sums(ni)
                with step.loop(0, KT // 2, 2 * NT) as i:
                    for j in range(2):
                        for tt in range(NT):
                            n = 2 * i + j
                            unit_wait(tt, DONE0[phase] + 2 * n + tt + 1, b0 + n)
                            xs = x[:, ds(n, 1), tt * TW:(tt + 1) * TW].rearrange("p a t -> p (a t)")
                            dve.tensor_tensor(xs, bank((OFF[phase] + 3 * j + tt) % 6), xs, ALU.add).then_inc(acc_free, 1)
                            dve.wait_ge(acc_free, FREE0[phase] + 3 * n + tt + 1)
                            add_squares(ni, n, tt, xs, tt % 2)

            def ffn(layer):
                c0 = FCH * layer

                def hidden(cx, par):
                    def low(v):
                        f, tt = v // 3, v % 3
                        dve.wait_ge(hh_ready, 6 * cx + v + 1)
                        dve.tensor_tensor(hl[:, par, f, tt * TW:(tt + 1) * TW], tmpb[:, v % 2, :],
                                          hh[:, par, f, tt * TW:(tt + 1) * TW].bitcast(F32),
                                          ALU.subtract).then_inc(hl_ready, 1)
                    for v in range(6):
                        dve.wait_ge(sil_ready, 6 * cx + v + 1)
                        if not (isinstance(cx, int) and v < 2):
                            dve.wait_ge(hl_ready, 6 * cx + v - 1)
                        dve.tensor_tensor(tmpb[:, v % 2, :], bank(2 * (v % 3) + 1), tmpa[:, v % 2, :],
                                          ALU.mult).then_inc(h32_ready, 1)
                        if v >= 1:
                            low(v - 1)
                    low(5)

                def add(cx, b):
                    for u in range(24):
                        mo, tt = u // 3, u % 3
                        if u % 12 == 11:
                            dve.wait_ge(block_done, done_count(b + u // 12))
                        else:
                            dve.wait_ge(down_done, 22 * cx + u + 1 - u // 12)
                        dve.wait_ge(down_added, DA + 24 * (cx - 1) + u + 1)
                        xs = x[:, mo, tt * TW:(tt + 1) * TW]
                        dve.tensor_tensor(xs, bank(u % 8), xs, ALU.add).then_inc(down_added, 1)

                b0 = (B0_FFN, B1_FFN)[layer]
                dve.wait_ge(xl_ready, 1 + XLN[f"ffn{layer}"] + KT * NT)
                hidden(c0, 0)
                with dve.Fori(0, FCH // 2) as i:
                    for j in range(2):
                        hidden(c0 + 1 + 2 * i + j, (j + 1) % 2)
                        add(c0 + 2 * i + j, b0 + 4 + 12 * i + 6 * j + 4)
                add(c0 + FCH - 1, b0 + B_FFN - 2)

            def ple(layer, b0):
                base_h = XLN[f"ple{layer}"]
                for kk in range(2):
                    dve.wait_ge(ph_ready, 2 * layer + kk + 1)
                    dve.tensor_tensor(pl[:, kk, :], praw[:, kk, :], ph[:, kk, :].bitcast(F32),
                                      ALU.subtract).then_inc(pl_ready, 1)
                for tt in range(NT):
                    for k in range(KT):
                        dve.wait_ge(xh_ready, base_h + KT * tt + k + 1)
                        sl = slice(tt * TW, (tt + 1) * TW)
                        dve.tensor_tensor(xl[:, k, sl], x[:, k, sl], xh[:, k, sl].bitcast(F32),
                                          ALU.subtract).then_inc(xl_ready, 1)
                free = FREE0[f"gate{layer}"]
                dve.wait_ge(acc_free, free)
                ni = 2 + 2 * layer
                clear_sums(ni)
                with step.loop(0, KT // 2, 2 * NT) as i:
                    for j in range(2):
                        for tt in range(NT):
                            n = 2 * i + j
                            u = 3 * j + tt
                            dve.wait_ge(sg_ready, 24 * layer + 3 * n + tt + 1)
                            dve.wait_ge(sq_added, 25 * (ni - 1) + 1 + 3 * n + tt)
                            sl = slice(tt * TW, (tt + 1) * TW)
                            pv = pp[:, ds(n, 1), sl].rearrange("p a t -> p (a t)")
                            xs = x[:, ds(n, 1), sl].rearrange("p a t -> p (a t)")
                            dve.tensor_tensor(tmpb[:, u % 2, :], tmpa[:, u % 2, :], pv, ALU.mult).then_inc(acc_free, 1)
                            dve.wait_ge(acc_free, free + 3 * n + tt + 1)
                            dve.tensor_tensor(xs, tmpb[:, u % 2, :], xs, ALU.add).then_inc(ple_added, 1)
                            dve.wait_ge(ple_added, 1 + 24 * layer + 3 * n + tt + 1)
                            add_squares(ni, n, tt, xs, u % 2)

            def log1p(z, e, q, p):
                step(dve.tensor_scalar(z, e, 2.0, None, ALU.add))
                step(dve.reciprocal(z, z))
                step(dve.tensor_tensor(z, z, e, ALU.mult))
                step(dve.tensor_tensor(q, z, z, ALU.mult))
                step(dve.tensor_scalar(p, q, 1.0 / 19.0, None, ALU.mult))
                for d in range(17, 1, -2):
                    step(dve.scalar_tensor_tensor(p, p, 1.0 / d, q, ALU.add, ALU.mult))
                step(dve.scalar_tensor_tensor(p, p, 1.0, z, ALU.add, ALU.mult))

            dve.memset(xh_flat[:, KT * TOK:XP].bitcast(F32), 0.0).then_inc(init_done, 1)
            dve.memset(xl_flat[:, KT * TOK:XP].bitcast(F32), 0.0).then_inc(init_done, 1)
            for t in range(AT):
                dve.memset(ua[:, t, 0:3], 0.0).then_inc(init_done, 1)
            dve.memset(kt[:, 0:P], 0.0).then_inc(init_done, 1)
            dve.memset(kt[:, 10 * P + TS:11 * P], 0.0).then_inc(init_done, 1)
            dve.memset(vtok[:, 0, :], 0.0).then_inc(init_done, 1)
            dve.memset(vtok[:, 10, :], 0.0).then_inc(init_done, 1)
            dve.wait_ge(const_in, 48)
            lam, (e_, z_, q_, p_, sp8, sp4, ab, mx) = vec("lam", 0, 4), [asmall[:, j, :] for j in range(8)]
            dve.scalar_tensor_tensor(ab, lam, -1.0, lam, ALU.mult, ALU.max).then_inc(lam_abs, 1)
            dve.wait_ge(lam_exp, 1)
            log1p(z_, e_, q_, p_)
            step(dve.tensor_scalar(mx, lam, -1.0, 0.0, ALU.mult, ALU.max))
            step(dve.scalar_tensor_tensor(mx, p_, 2.0, mx, ALU.mult, ALU.add))
            dve.tensor_scalar(sp4, mx, 4.0, None, ALU.mult).then_inc(sp_ready, 1)
            dve.tensor_scalar(sp8, mx, -8.0, None, ALU.mult).then_inc(sp_ready, 1)
            norm(0)

            dve.wait_ge(acc_free, FREE0["in0"] + 3 * 8)
            dve.wait_ge(v_ready, 3)
            dve.wait_ge(kv_sent, 48)
            dve.wait_ge(m0_in, 16 * 5)
            dve.wait_ge(init_done, 2 + AT + 4)

            def conv(t):
                cv = uc[t % 2]
                step(dve.tensor_scalar(cv[:, :], ua[:, t, 0:CA], vec("a_w", t), vec("a_b", t), ALU.mult, ALU.add))
                for j in range(1, 4):
                    ins = dve.scalar_tensor_tensor(cv[:, :], ua[:, t, j:j + CA], vec("a_w", 4 * j + t), cv[:, :],
                                                   ALU.mult, ALU.add)
                    if j < 3:
                        step(ins)
                    else:
                        ins.then_inc(uc_ready, 1)

            conv(0)
            for t in range(AT):
                dve.wait_ge(uc_ready, t + 1)
                dve.wait_ge(gate_out, 6 * t + 6)
                dve.tensor_tensor(lr3[:, :], lr3[:, :], uc[t % 2][:, :], ALU.mult).then_inc(iu_done, 1)
                if t < AT - 1:
                    conv(t + 1)
                dve.wait_ge(et_ready, 2 * t + 2)
                step(dve.tensor_scalar(lr2[:, :], lr2[:, :], 0.5, 0.5, ALU.mult, ALU.add))
                step(dve.scalar_tensor_tensor(lr4[:, :], lr1[:, :], 1.0, lr2[:, :], ALU.add, ALU.mult))
                step(dve.scalar_tensor_tensor(lr4[:, :], lr4[:, :], 2.0, lr2[:, :], ALU.subtract, ALU.mult))
                dve.wait_ge(sq4_ready, t + 1)
                step(dve.scalar_tensor_tensor(lr1[:, :], lr1[:, :], 1.0, lr4[:, :], ALU.subtract, ALU.mult))
                step(dve.scalar_tensor_tensor(lr2[:, :], uc[t % 2][:, :], -1.0, lr4[:, :], ALU.mult, ALU.mult))
                dve.wait_ge(iu_done, t + 1)
                step(dve.tensor_tensor(lr2[:, :], lr2[:, :], lr3[:, :], ALU.mult))
                dve.wait_ge(aconv_sent, 32)
                step(dve.tensor_tensor_scan(ua[:, t, 0:TP], lr1[:, 0:TP], lr2[:, 0:TP], 0.0, ALU.mult, ALU.add))
                dve.tensor_tensor_scan(ua[:, t, SA:CA], lr1[:, SA:CA], lr2[:, SA:CA], vec("h0", t),
                                       ALU.mult, ALU.add).then_inc(h_ready, 1)
            dve.wait_ge(block_done, done_count(B0_OUT - 1))
            dve.wait_ge(acc_free, FREE0["in0"] + 42)
            dve.wait_ge(h_ready, AT)

            def y_low(t):
                dve.wait_ge(yh_ready, t + 1)
                yb = (lr1, lr2)[t % 2]
                dve.tensor_tensor(xl[:, t, :], yb[:, 0:TOK], xh[:, t, :].bitcast(F32),
                                  ALU.subtract).then_inc(yl_ready, 1)

            for t in range(AT):
                yb = (lr1, lr2)[t % 2]
                if t >= 2:
                    dve.wait_ge(yl_ready, t - 1)
                step(dve.tensor_tensor(yb[:, 0:TP], ua[:, t, 0:TP], ga[:, t, 0:TP], ALU.mult))
                dve.tensor_tensor(yb[:, TP:TOK], ua[:, t, SA:CA], ga[:, t, TP:TOK], ALU.mult).then_inc(y_ready, 1)
                dve.wait_ge(y_ready, t + 1)
                if t >= 1:
                    y_low(t - 1)
            y_low(AT - 1)
            dve.wait_ge(ah_kept, 2)
            dve.wait_ge(yl_ready, AT)

            def before(n, kvh, var):
                dve.wait_ge(s_done, 2 * n + kvh + 1)
                if not (isinstance(n, int) and n == 0):
                    dve.wait_ge(pt_done, 2 * n + kvh - 1)
                for g in range(4):
                    sps = ps[:, 2 * kvh + g // 2, (g % 2) * 256:(g % 2) * 256 + 256]
                    ins = dve.scalar_tensor_tensor(ss[:, kvh, g, :], dist[:, var, :], -8.0 * SLOPE[4 * kvh + g],
                                                   sps, ALU.mult, ALU.add)
                    if g < 3:
                        step.mark(ins)
                    else:
                        ins.then_inc(s_read, 1)
                step.wait()
                dve.wait_ge(s_read, 2 * n + kvh + 1)
                w = [sm[:, kvh, j, :] for j in range(6)]
                step(dve.tensor_reduce(w[0], ss[:, kvh, :, :], AX.X, ALU.max))
                step(dve.scalar_tensor_tensor(w[0], w[0], 0.125, vec("sink", 4 * kvh, 4), ALU.mult, ALU.max))
                step(dve.tensor_scalar(w[1], w[0], -1.0, None, ALU.mult))
                dve.tensor_tensor(w[2], vec("sink", 4 * kvh, 4), w[0], ALU.subtract).then_inc(nm_ready, 1)

            def sums(n, kvh):
                w = [sm[:, kvh, j, :] for j in range(6)]
                dve.wait_ge(exp_done, 2 * n + kvh + 1)
                step(dve.tensor_tensor(w[4], w[4], w[3], ALU.add))
                step(dve.reciprocal(w[5], w[4]))

            def after(n, kvh):
                dve.wait_ge(o_done, 2 * n + kvh + 1)
                if kvh == 0 and not (isinstance(n, int) and n == 0):
                    dve.wait_ge(ot_done, n)
                ov = ps[:, 6, :].rearrange("p (g a d) -> p g a d", g=4, a=2)[:, :, kvh, :]
                dve.tensor_tensor(otok[:, :, kvh, :], ov,
                                  sm[:, kvh, 5, :].rearrange("p (g o) -> p g o", o=1).to_broadcast([P, 4, HD]),
                                  ALU.mult).then_inc(o_read, 1)

            def out_low(n, col, width):
                dve.wait_ge(oh_ready, n + 1)
                ov = ps[:, 7, :].rearrange("p (g t) -> p g t", g=4)[:, :, 0:width]
                dve.tensor_tensor(xl[:, 4:8, ds(col, width)], ov, xh[:, 4:8, ds(col, width)].bitcast(F32),
                                  ALU.subtract).then_inc(ol_ready, 1)

            def attend(n, var, last=None):
                if not (isinstance(n, int) and n == 0):
                    sums(n - 1, 1)
                before(n, 1, 2 if isinstance(n, int) and n == NQ - 1 else 0 if isinstance(n, int) and n == 0 else 1)
                if not (isinstance(n, int) and n == 0):
                    after(n - 1, 1)
                sums(n, 0)
                if var is not None:
                    before(n + 1, 0, var)
                after(n, 0)
                if last is not None:
                    out_low(n - 1, *last)

            before(0, 0, 0)
            attend(0, 1)
            with step.loop(1, NQ - 3, 2 * (2 + 6)) as i:
                attend(i, 1, (i * P - P, P))
            attend(NQ - 3, 1, ((NQ - 4) * P, P))
            attend(NQ - 2, 2, ((NQ - 3) * P, P))
            attend(NQ - 1, None, ((NQ - 2) * P, P))
            sums(NQ - 1, 1)
            after(NQ - 1, 1)
            out_low(NQ - 1, TP, TS)
            dve.wait_ge(x_in, 16 * 2)
            add_loop("out0", B0_OUT, 1)
            norm(1)
            ffn(0)
            ple(0, B0_PLE)
            norm(2)
            dve.wait_ge(x_saved, 16)
            dve.wait_ge(xl_ready, 1 + XLN["mix1"] + KT * NT)
            dve.memset(uu[:, :, 0:3], 0.0).then_inc(pads_ready, 1)
            dve.memset(uu[:, :, 6 + TOK:UC], 0.0).then_inc(pads_ready, 1)

            R = [rows[:, j, :] for j in range(6)]
            for tt in range(NT):
                unit_wait(tt, DONE0["g1"] + tt + 1, B1_GATE)
                sl = slice(tt * TW, (tt + 1) * TW)
                step.mark(dve.tensor_scalar(rows[:, 0, sl], ps[0:4, tt, 0:TW], vecs[0:4, VEC["b_gate"]:VEC["b_gate"] + 1],
                                            None, ALU.add))
                dve.tensor_scalar(rows[:, 1, sl], ps[32:36, tt, 0:TW], vecs[32:36, VEC["b_gate"]:VEC["b_gate"] + 1],
                                  None, ALU.add).then_inc(acc_free, 1)
            step(dve.memset(rows[:, 0, TOK:CH * P], NEG))
            step(dve.memset(rows[:, 1, TOK:CH * P], 0.0))
            dve.wait_ge(acc_free, FREE0["g1"] + 3)
            dve.scalar_tensor_tensor(R[2], R[1], -1.0, R[1], ALU.mult, ALU.max).then_inc(fabs_ready, 1)
            dve.wait_ge(fexp_ready, 1)
            log1p(R[3], R[2], R[4], R[5])
            step(dve.tensor_scalar(R[1], R[1], 0.0, None, ALU.min))
            step(dve.scalar_tensor_tensor(R[1], R[5], -2.0, R[1], ALU.mult, ALU.add))
            step(dve.memset(R[5], 1.0))
            step(dve.memset(rows[:, 5, 0:CH * P:P], 0.0))
            step(dve.tensor_tensor_scan(R[2], R[5], R[1], 0.0, ALU.mult, ALU.add))
            step(dve.tensor_tensor_scan(rows[:, 3, 0:TP], rows[:, 1, 0:TP], rows[:, 0, 0:TP], 0.0, ALU.add, ALU.max))
            step(dve.tensor_tensor_scan(rows[:, 3, TP:CH * P], rows[:, 1, TP:CH * P], rows[:, 0, TP:CH * P],
                                        vecs[0:4, VEC["m0"]:VEC["m0"] + 1], ALU.add, ALU.max))
            step(dve.tensor_tensor(R[0], R[0], R[2], ALU.subtract))
            step(dve.tensor_tensor(arow[:, :], R[2], R[3], ALU.subtract))
            step(dve.tensor_copy(rsmall[:, 16:24], arow[:, P - 1:TP:P]))
            step(dve.tensor_copy(rsmall[:, 24:25], arow[:, TOK - 1:TOK]))
            step(dve.memset(rsmall[:, 48:49], 0.0))
            step(dve.tensor_copy(rsmall[:, 49:56], rows[:, 3, P - 1:TP - P:P]))
            step(dve.tensor_copy(rsmall[:, 56:57], vecs[0:4, VEC["m0"]:VEC["m0"] + 1]))

            def bc(v):
                return v.rearrange("p (c o) -> p c o", o=1).to_broadcast([4, CH, P])

            def by_chunk(v):
                return v.rearrange("p (c t) -> p c t", c=CH)

            step(dve.tensor_tensor(by_chunk(R[5]), by_chunk(arow[:, :]), bc(rsmall[:, 48:57]), ALU.add))
            step(dve.tensor_tensor(by_chunk(R[1]), by_chunk(R[0]), bc(rsmall[:, 16:25]), ALU.add))
            dve.tensor_tensor(rsmall[:, 32:41], rsmall[:, 16:25], rsmall[:, 48:57], ALU.add).then_inc(rows_log, 1)

            dve.wait_ge(cols_out, 2)
            dve.wait_ge(acc_free, FREE0["u1"] + 24)
            dve.wait_ge(cconv_sent, 32)
            dve.wait_ge(pads_ready, 2)
            dve.wait_ge(c_in, 16 * 4)
            with step.loop(0, KT // 2, 2 * 3) as i:
                for j in range(2):
                    n = 2 * i + j
                    dve.wait_ge(silu_done, n + 1)
                    cv = ct[j][:, :]

                    def uv(o):
                        return uu[:, ds(n, 1), o:o + CC].rearrange("p a t -> p (a t)")

                    def cvec(name, o):
                        return vecs[:, ds(VEC[name] + o + n, 1)]

                    step(dve.tensor_scalar(cv, uv(0), cvec("c_w", 0), cvec("c_b", 0), ALU.mult, ALU.add))
                    for o in range(1, 4):
                        ins = dve.scalar_tensor_tensor(cv, uv(o), cvec("c_w", 8 * o), cv, ALU.mult, ALU.add)
                        if o < 3:
                            step(ins)
                        else:
                            ins.then_inc(ct_ready, 1)
            dve.wait_ge(silu_done, KT + 2)
            dve.memset(cs[:, :, :, :].rearrange("p h k e -> p (h k e)"), 0.0).then_inc(c_zero, 1)
            dve.memset(vb[:, :, HC:HC + 1], 1.0).then_inc(c_zero, 1)
            dve.wait_ge(c_zero, 2)

            def decays(n):
                dve.wait_ge(ab_done, n + 1)
                dve.tensor_tensor(dw[:, :, :], ps[:, 4, :].rearrange("p (h t) -> p h t", h=H),
                                  cmask[:, :].rearrange("p (o t) -> p o t", o=1).to_broadcast([P, H, P]),
                                  ALU.add).then_inc(dwm_ready, 1)

            def weigh(n):
                dve.wait_ge(dw_ready, n + 1)
                dve.wait_ge(st_done, n + 1)
                dve.tensor_tensor(sw[:, :, :].rearrange("p h t -> p (h t)"), ps[:, 5, :],
                                  dw[:, :, :].rearrange("p h t -> p (h t)"), ALU.mult).then_inc(sw_ready, 1)

            def out_low(n, col, width):
                dve.wait_ge(ch_ready, n + 1)
                for t in range(KT):
                    ins = dve.scalar_tensor_tensor(xl[:, t, ds(col, width)],
                                                   ps[:, 6 + t // 4, (t % 4) * P:(t % 4) * P + width], vec("c_g", t),
                                                   xh[:, t, ds(col, width)].bitcast(F32), ALU.mult, ALU.subtract)
                    if t < KT - 1:
                        step.mark(ins)
                    else:
                        ins.then_inc(cl_ready, 1)

            def update(n, u):
                dve.wait_ge(cup_done, 8 * n + u + 1)
                csv = cs[:, u // 2, u % 2, :]
                dve.scalar_tensor_tensor(csv, csv, decay_col(n, u // 2), bank((0, 1, 4, 5)[u % 4], HC + 1),
                                         ALU.mult, ALU.add).then_inc(cup_read, 1)

            def normalise(h):
                dve.tensor_scalar(hb[:, h, :], hb[:, h, :], st[:, 24 + 2 * h:25 + 2 * h], st[:, 44 + h:45 + h],
                                  ALU.subtract, ALU.mult).then_inc(hb_ready, 1)

            def chunk(n, last, nxt):
                for h in range(H):
                    dve.wait_ge(iq_ready, 4 * n + h + 1)
                    dve.tensor_tensor(iq[:, h, :], bank((6, 2)[h % 2], HC + 1), iq[:, h, :],
                                      ALU.add).then_inc(num_read, 1)
                    if last is not None:
                        normalise(h)
                dve.wait_ge(num_read, 1 + 4 * n + 4)
                step(dve.scalar_tensor_tensor(st[:, 32:36], iq[:, :, HC], -1.0, iq[:, :, HC], ALU.mult, ALU.max))
                step(dve.tensor_tensor(st[:, 32:36], st[:, 32:36],
                                       cols[:, ds(n, 1), 2, :].rearrange("p a h -> p (a h)"), ALU.max))
                step(dve.reciprocal(st[:, 36:40], st[:, 32:36]))
                for u in range(2):
                    update(n, u)
                dve.wait_ge(o_in, 16 * (n + 1))
                dve.wait_ge(htr_done, 1 + n)
                for h in range(H):
                    step.mark(dve.scalar_tensor_tensor(hb[:, h, :], iq[:, h, 0:HC], st[:, 36 + h:37 + h],
                                                       ob[:, h, :], ALU.mult, ALU.mult))
                for u in range(2, 4):
                    update(n, u)
                if last is not None:
                    out_low(*last)
                for u in range(4, 8):
                    update(n, u)
                step.wait()
                for h in range(H):
                    step.mark(dve.bn_stats(st[:, 6 * h:6 * h + 6], hb[:, h, :]))
                step.wait()
                if nxt is not None:
                    decays(nxt)
                for h in range(H):
                    dve.bn_aggr(st[:, 24 + 2 * h:26 + 2 * h], st[:, 6 * h:6 * h + 6]).then_inc(var_ready, 1)
                if nxt is not None:
                    weigh(nxt)
                dve.wait_ge(sd_ready, n + 1)
                step(dve.reciprocal(st[:, 44:48], st[:, 40:44]))

            def decay_col(n, h):
                return decay[:, ds(n, 1), h:h + 1].rearrange("p a h -> p (a h)")

            decays(0)
            weigh(0)
            chunk(0, None, 1)
            with step.loop(1, CH - 2, 3 + 4 + 4 + 1 + 7) as i:
                chunk(i, (i - 1, i * P - P, P), i + 1)
            chunk(CH - 2, (CH - 3, (CH - 3) * P, P), CH - 1)
            dve.wait_ge(c_swap, 16)
            chunk(CH - 1, (CH - 2, (CH - 2) * P, P), None)
            for h in range(H):
                normalise(h)
            out_low(CH - 1, TP, TS)
            dve.wait_ge(x_in, 16 * 3)
            add_loop("out1", B1_OUT, 3)
            norm(3)
            ffn(1)
            ple(1, B1_PLE)

            dve.wait_ge(ple_added, 1 + 48)
            for tt in range(NT):
                rstd_of(4, tt)
                dve.wait_ge(rstd_ready, 1 + 12 + tt + 1)
                sl = slice(tt * TW, (tt + 1) * TW)
                for k in range(KT):
                    dve.scalar_tensor_tensor(ybuf[:, k, sl], x[:, k, sl], vec("g_fin", k),
                                             rstd[:, :], ALU.mult, ALU.mult).then_inc(xt_ready, 1)

        @block.scalar
        def _(act):
            def squares(tt):
                act.wait_ge(xt_in[tt], 16)
                act.wait_ge(ss_done, 1 + tt)
                sl = slice(tt * TW, (tt + 1) * TW)
                for k in range(KT):
                    act.activation(sqx[:, (KT * tt + k) % 12, :], x[:, k, sl], ACT.Square).then_inc(sq_ready, 1)

            def root(ni, tt):
                g = 3 * ni + tt
                act.wait_ge(ss_done, 1 + g + 1)
                act.wait_ge(rstd_ready, 1 + g)
                act.activation(rt[:, :], bank(6 + tt % 2), ACT.Sqrt, bias=vec("eps"), scale=1.0 / D).then_inc(rt_ready, 1)

            def high(ni, tt, k):
                act.wait_ge(xt_ready, 1 + KT * (3 * ni + tt) + k + 1)
                act.activation(xh[:, k, tt * TW:(tt + 1) * TW], tmp[:, k % 4, :], ACT.Copy).then_inc(xh_ready, 1)

            def input_norm():
                act.wait_ge(xt_in[0], 16)
                load_x(1)
                squares(0)
                load_x(2)
                act.dma_start(ua[:, :, 3 + TP:6 + TP], I["a_conv"]).then_inc(m0_in, 16)
                act.dma_start(lbd[:, :, :, :], I["lbd"]).then_inc(m0_in, 16)
                act.dma_start(dist[:, :, :], I["dist"]).then_inc(m0_in, 16)
                act.dma_start(kt[:, 9 * P:10 * P], I["kc"]).then_inc(m0_in, 16)
                act.dma_start(vtok[:, 9, :], I["vc"]).then_inc(m0_in, 16)
                root(0, 0)
                squares(1)
                for tt in range(NT):
                    for k in range(KT):
                        high(0, tt, k)
                        if k == KT // 2 and tt < NT - 1:
                            root(0, tt + 1)
                    if tt == 0:
                        squares(2)

            def norm(ni):
                root(ni, 0)
                for tt in range(NT):
                    for k in range(KT):
                        high(ni, tt, k)
                        if k == KT // 2 and tt < NT - 1:
                            root(ni, tt + 1)

            def ffn(layer):
                c0 = FCH * layer

                def hidden(cx, b, par, outs):
                    if outs:
                        act.wait_ge(down_added, DA + 24 * (cx - 1))

                    def high(v):
                        f, tt = v // 3, v % 3
                        act.wait_ge(h32_ready, 6 * cx + v + 1)
                        act.activation(hh[:, par, f, tt * TW:(tt + 1) * TW], tmpb[:, v % 2, :],
                                       ACT.Copy).then_inc(hh_ready, 1)
                    for v in range(6):
                        f, tt = v // 3, v % 3
                        if tt < 2:
                            act.wait_ge(pair_done, 4 * cx + 2 * f + tt + 1)
                        else:
                            act.wait_ge(block_done, done_count(b + 2 * f + 1))
                        act.activation(tmpa[:, v % 2, :], bank(2 * tt), ACT.Silu).then_inc(sil_ready, 1)
                        if v >= 1:
                            high(v - 1)
                    high(5)

                b0 = (B0_FFN, B1_FFN)[layer]
                act.wait_ge(xl_ready, 1 + XLN[f"ffn{layer}"] + KT * NT)
                hidden(c0, b0, 0, False)
                with act.Fori(0, FCH // 2) as i:
                    for j in range(2):
                        hidden(c0 + 1 + 2 * i + j, b0 + 4 + 12 * i + 6 * j, (j + 1) % 2, True)

            def ple(layer, b0):
                act.wait_ge(p_in, 16 * (layer + 1))
                for kk in range(2):
                    act.activation(ph[:, kk, :], praw[:, kk, :], ACT.Copy).then_inc(ph_ready, 1)
                act.wait_ge(down_added, DA + 24 * FCH * (layer + 1))
                off = OFF[f"proj{layer}"]
                for tt in range(NT):
                    sl = slice(tt * TW, (tt + 1) * TW)
                    for k in range(KT):
                        act.activation(xh[:, k, sl], x[:, k, sl], ACT.Copy).then_inc(xh_ready, 1)
                    for mo in range(KT):
                        u = KT * tt + mo
                        if u < 23:
                            act.wait_ge(acc_done, DONE0[f"proj{layer}"] + u + 1)
                        else:
                            act.wait_ge(block_done, done_count(b0 + 1))
                        act.activation(pp[:, mo, sl], bank((u + off) % 6), ACT.Copy).then_inc(acc_free, 1)
                with act.Fori(0, KT // NW) as i:
                    for j in range(NW):
                        for tt in range(NT):
                            n = NW * i + j
                            u = 3 * j + tt
                            unit_wait(tt, DONE0[f"gate{layer}"] + 2 * n + tt + 1, b0 + 2 + n)
                            act.wait_ge(acc_free, FREE0[f"gate{layer}"] + 3 * n + tt - 1)
                            act.activation(tmpa[:, u % 2, :], bank((OFF[f"gate{layer}"] + u) % 6),
                                           ACT.Sigmoid).then_inc(sg_ready, 1)

            def unit_wait(tt, done, b):
                if tt < NT - 1:
                    act.wait_ge(acc_done, done)
                else:
                    act.wait_ge(block_done, done_count(b))

            def load_x(tt):
                sl = slice(tt * TW, (tt + 1) * TW)
                act.dma_start(x[:, :, sl], I["xT"][:, :, sl]).then_inc(xt_in[tt], 16)

            act.dma_start(vecs[:, :], I["vecs"]).then_inc(const_in, 16)
            load_x(0)
            act.dma_start(ones[:, :], I["ones"]).then_inc(const_in, 16)
            act.dma_start(ident[:, :], I["ident"]).then_inc(const_in, 16)
            act.wait_ge(lam_abs, 1)
            act.activation(asmall[:, 0, :], asmall[:, 6, :], ACT.Exp, scale=-1.0).then_inc(lam_exp, 1)
            input_norm()

            def copy_out(j):
                for tt in range(NT):
                    unit_wait(tt, DONE0["in0"] + 2 * j + tt + 1, B0_IN + j)
                    src = bank((OFF["in0"] + 3 * j + tt) % 6)
                    if j < 5:
                        dst, sample = (ua[:, j, :], 6 + TP) if j < 4 else (kt[:, :], 10 * P)
                        off = 3 if j < 4 else P
                        if tt < NT - 1:
                            act.activation(dst[:, off + tt * TW:off + (tt + 1) * TW], src, ACT.Copy).then_inc(acc_free, 1)
                        else:
                            act.activation(dst[:, off + tt * TW:off + TP], src[:, 0:LAST], ACT.Copy)
                            act.activation(dst[:, sample:sample + TS], src[:, LAST:TW], ACT.Copy).then_inc(acc_free, 1)
                        continue
                    sl = slice(tt * TW, (tt + 1) * TW)
                    if j == 5:
                        act.activation(vt[:, sl], src, ACT.Copy).then_inc(acc_free, 1)
                    elif j < 10:
                        act.activation(qt0[:, j - 6, sl], src, ACT.Copy).then_inc(acc_free, 1)
                    else:
                        act.activation(ga[:, j - 10, sl], src, ACT.Gelu_apprx_tanh).then_inc(acc_free, 1)

            def lru(t):
                act.wait_ge(h_ready, t)
                for u in range(6):
                    act.wait_ge(gate_done, 6 * t + u + 1)
                    dst, b = ((lr1, "b_r"), (lr3, "b_i"))[u // 3]
                    sl = slice((u % 3) * 353, (u % 3 + 1) * 353)
                    act.activation(dst[:, sl], bank(6 + u % 2, 353), ACT.Sigmoid, bias=vec(b, t)).then_inc(gate_out, 1)
                act.wait_ge(gate_out, 6 * t + 6)
                act.activation(lr2[:, :], lr1[:, :], ACT.Exp, scale=asmall[:, 4, t:t + 1]).then_inc(et_ready, 1)
                act.activation(lr1[:, :], lr1[:, :], ACT.Tanh, scale=asmall[:, 5, t:t + 1]).then_inc(et_ready, 1)
                act.wait_ge(et_ready, 2 * t + 2)
                act.wait_ge(iu_done, t + 1)
                act.activation(uc[t % 2][:, :], lr1[:, :], ACT.Sqrt, scale=4.0).then_inc(sq4_ready, 1)

            act.wait_ge(m0_in, 16 * 5)
            act.wait_ge(init_done, 2 + AT + 4)
            for j in range(8):
                copy_out(j)
                if j == 4:
                    act.wait_ge(acc_free, FREE0["in0"] + 15)
                    act.dma_start(O["a_conv_o"][:, :, 0:3], ua[:, :, TP:TP + 3]).then_inc(aconv_sent, 16)
                    act.dma_start(O["a_conv_o"][:, :, 3:6], ua[:, :, UA - 3:UA]).then_inc(aconv_sent, 16)
                    act.dma_start(O["k_o"][:, 0:P], kt[:, TP:TP + P]).then_inc(kv_sent, 16)
                    act.dma_start(O["k_o"][:, P:P + TS], kt[:, 10 * P:10 * P + TS]).then_inc(kv_sent, 16)
                if j == 6:
                    act.wait_ge(acc_free, FREE0["in0"] + 18)
                    act.dma_start(O["v_o"], vt[:, TOK - P - TS:TOK]).then_inc(kv_sent, 16)
            for j in range(3):
                act.wait_ge(vtr_done, j + 1)
                if j < 2:
                    act.activation(vtok[:, 4 * j + 1:4 * j + 5, :].rearrange("p a d -> p (a d)"), ps[:, 7, :],
                                   ACT.Copy).then_inc(v_ready, 1)
                else:
                    act.activation(vtok[0:TS, 10, :], ps[0:TS, 7, 0:P], ACT.Copy).then_inc(v_ready, 1)
            act.wait_ge(sp_ready, 2)
            for j in range(8, 14):
                copy_out(j)
                if 8 <= j < 12:
                    lru(j - 8)
            act.wait_ge(h_ready, AT)
            act.activation(asmall[:, 2, :], ua[:, :, TP - 1], ACT.Copy).then_inc(ah_kept, 1)
            act.activation(asmall[:, 3, :], ua[:, :, CA - 1], ACT.Copy).then_inc(ah_kept, 1)
            act.wait_ge(ah_kept, 2)
            act.dma_start(O["a_h_o"], asmall[:, 2:4, :]).then_inc(ah_sent, 16)
            act.wait_ge(block_done, done_count(B0_OUT - 1))
            for t in range(AT):
                act.wait_ge(y_ready, t + 1)
                act.activation(xh[:, t, :], (lr1, lr2)[t % 2][:, 0:TOK], ACT.Copy).then_inc(yh_ready, 1)
            act.wait_ge(yl_ready, AT)
            act.dma_start(x[:, 0:4, :], I["xT"][:, 0:4, :]).then_inc(x_in, 16)

            def stage_qk(n, col, width, kcol):
                if not (isinstance(n, int) and n == 0):
                    act.wait_ge(s_done, 2 * n)
                act.activation(qs[:, :, 0:width], qt0[:, :, ds(col, width)], ACT.Copy).then_inc(qk_staged, 1)
                act.activation(ks[:, :], kt[:, ds(kcol, 2 * P)], ACT.Copy).then_inc(qk_staged, 1)

            def exps(n, kvh):
                act.wait_ge(nm_ready, 2 * n + kvh + 1)
                act.activation(sm[:, kvh, 3, :], sm[:, kvh, 2, :], ACT.Exp)
                for g in range(4):
                    ins = act.activation(ss[:, kvh, g, :], ss[:, kvh, g, :], ACT.Exp, bias=sm[:, kvh, 1, g:g + 1],
                                         scale=0.125, accum_out=sm[:, kvh, 4, g:g + 1])
                ins.then_inc(exp_done, 1)

            def copy_p(n, kvh):
                act.wait_ge(pt_done, 2 * n + kvh + 1)
                if not (isinstance(n, int) and n == 0 and kvh == 0):
                    act.wait_ge(o_done, 2 * n + kvh)
                act.activation(pts[:, :, :].rearrange("p a q -> p (a q)"),
                               ps[:, 4:6, :].rearrange("p b q -> p (b q)"), ACT.Copy).then_inc(pt_out, 1)

            def out_high(n, col, width):
                act.wait_ge(ot_done, n + 1)
                act.activation(xh[:, 4:8, ds(col, width)],
                               ps[:, 7, :].rearrange("p (g t) -> p g t", g=4)[:, :, 0:width],
                               ACT.Copy).then_inc(oh_ready, 1)

            def attend(n, staged, last):
                if not (isinstance(n, int) and n == 0):
                    copy_p(n - 1, 1)
                exps(n, 1)
                copy_p(n, 0)
                if staged is not None:
                    stage_qk(n + 2, *staged)
                if last is not None:
                    out_high(n - 1, *last)
                if not (isinstance(n, int) and n == NQ - 1):
                    exps(n + 1, 0)

            stage_qk(0, 0, P, 0)
            stage_qk(1, P, P, P)
            exps(0, 0)
            attend(0, (2 * P, P, 2 * P), None)
            with act.Fori(1, NQ - 3) as i:
                attend(i, (i * P + 2 * P, P, i * P + 2 * P), (i * P - P, P))
            attend(NQ - 3, (TP, TS, 9 * P), ((NQ - 4) * P, P))
            attend(NQ - 2, None, ((NQ - 3) * P, P))
            act.dma_start(x[:, 4:8, :], I["xT"][:, 4:8, :]).then_inc(x_in, 16)
            attend(NQ - 1, None, ((NQ - 2) * P, P))
            copy_p(NQ - 1, 1)
            out_high(NQ - 1, TP, TS)
            act.wait_ge(ol_ready, NQ)
            act.dma_start(praw[:, :, :], I["pT"][0]).then_inc(p_in, 16)
            act.wait_ge(acc_free, FREE0["out0"] + 24)
            norm(1)
            ffn(0)
            ple(0, B0_PLE)

            act.wait_ge(ple_added, 1 + 24)
            act.dma_start(xsave, x[:, :, :]).then_inc(x_saved, 16)
            act.dma_start(cbd[:, :, :, :], I["cbd"]).then_inc(c_in, 16)
            act.dma_start(sel[:, :, :], I["sel"]).then_inc(c_in, 16)
            act.dma_start(cmask[:, :], I["cmask"]).then_inc(c_in, 16)
            norm(2)
            act.wait_ge(x_saved, 16)
            act.wait_ge(xl_ready, 1 + XLN["mix1"] + KT * NT)
            act.dma_start(uu[:, :, 3 + TP:6 + TP], I["c_conv"]).then_inc(c_in, 16)
            act.wait_ge(c_in, 64)
            act.wait_ge(pads_ready, 2)

            def u_out(n, j):
                for tt in range(NT):
                    unit_wait(tt, DONE0["u1"] + 2 * n + tt + 1, B1_U + n)
                    src = bank((OFF["u1"] + 3 * j + tt) % 6)
                    dst = uu[:, ds(n, 1), :].rearrange("p a t -> p (a t)")
                    if tt < NT - 1:
                        act.activation(dst[:, 3 + tt * TW:3 + (tt + 1) * TW], src, ACT.Copy).then_inc(acc_free, 1)
                    else:
                        act.activation(dst[:, 3 + tt * TW:3 + TP], src[:, 0:LAST], ACT.Copy)
                        act.activation(dst[:, 6 + TP:6 + TOK], src[:, LAST:TW], ACT.Copy).then_inc(acc_free, 1)

            def row_exps():
                act.wait_ge(rows_log, 1)
                act.activation(rsmall[:, 60:62], rows[:, 3, TP - 1:TOK:TS], ACT.Copy).then_inc(m_kept, 1)
                act.wait_ge(m_kept, 1)
                act.dma_start(O["m_o"], rsmall[:, 60:62]).then_inc(m_sent, 16)
                act.activation(rows[:, 4, :], rows[:, 3, :], ACT.Exp, scale=-1.0)
                act.activation(rows[:, 5, :], rows[:, 5, :], ACT.Exp)
                act.activation(rows[:, 1, :], rows[:, 1, :], ACT.Exp)
                act.activation(rsmall[:, 32:41], rsmall[:, 32:41], ACT.Exp).then_inc(rows_ready, 1)

            act.wait_ge(fabs_ready, 1)
            act.activation(rows[:, 2, :], rows[:, 2, :], ACT.Exp, scale=-1.0).then_inc(fexp_ready, 1)
            with act.Fori(0, KT // NW) as i:
                for j in range(NW):
                    u_out(NW * i + j, j)
            act.wait_ge(acc_free, FREE0["u1"] + 24)
            act.activation(seeds[:, 5:6], seeds[:, 0:1], ACT.Copy).then_inc(block_done, 1)
            act.dma_start(O["c_conv_o"][:, :, 0:3], uu[:, :, TP:TP + 3]).then_inc(cconv_sent, 16)
            act.dma_start(O["c_conv_o"][:, :, 3:6], uu[:, :, 3 + TOK:6 + TOK]).then_inc(cconv_sent, 16)
            row_exps()
            act.wait_ge(cols_done, 1)
            act.activation(cols[:, :, :, :].rearrange("p c q h -> p (c q h)"), ps[:, 6, 0:CH * 4 * H],
                           ACT.Copy).then_inc(cols_out, 1)
            act.activation(decay[:, :, :].rearrange("p c h -> p h c"),
                           ps[:, 6, 256:256 + CH * H].rearrange("p (h c) -> p h c", h=H), ACT.Copy).then_inc(cols_out, 1)

            def silu(n, j):
                act.wait_ge(ct_ready, n + 1)
                act.activation(uu[:, ds(n, 1), 0:CC].rearrange("p a t -> p (a t)"), ct[j][:, :],
                               ACT.Silu).then_inc(silu_done, 1)

            def vo_out(pair, pr, it, func, j):
                u = CH * pr + j
                if j < CH - 1:
                    act.wait_ge(acc_done, DONE0["vo1"] + 8 * pair + j + 1)
                else:
                    act.wait_ge(block_done, done_count(B1_VO + 2 * pair + 1))
                act.wait_ge(stage_out[u % 2], 16 + 16 * (CH * it + u // 2))
                act.activation(stage[:, u % 2, :], ps[:, (u + OFF["vo1"]) % 6, 0:2 * P], func).then_inc(acc_free, 1)
                act.wait_ge(acc_free, FREE0["vo1"] + CH * pair + j + 1)
                act.dma_start(vod[j, :, ds(pair * 2 * P, 2 * P)], stage[:, u % 2, :]).then_inc(stage_out[u % 2], 16)

            for half, func in ((0, ACT.Copy), (1, ACT.Sigmoid)):
                with act.Fori(0, 2) as i:
                    for pr in range(2):
                        for j in range(CH):
                            vo_out(4 * half + 2 * i + pr, pr, 2 * half + i, func, j)
                            if half == 0 and j in (3, 7):
                                silu(4 * i + 2 * pr + j // 4, j // 4)

            def load_v(n):
                act.dma_start(vb[:, :, 0:HC], vod[n, :, 0:D].rearrange("p (h e) -> p h e", h=H)
                              if isinstance(n, int) else
                              vod[ds(n, 1), :, 0:D].rearrange("a p (h e) -> (a p) h e", h=H)).then_inc(v_in, 16)

            def load_o(n):
                act.dma_start(ob[:, :, :], vod[n, :, D:2 * D].rearrange("p (h e) -> p h e", h=H)
                              if isinstance(n, int) else
                              vod[ds(n, 1), :, D:2 * D].rearrange("a p (h e) -> (a p) h e", h=H)).then_inc(o_in, 16)

            def keys_queries(n):
                for w, (dst, sc, b0) in enumerate(((ck, HC ** -0.5, 2), (cq, 1.0, 6))):
                    act.wait_ge(qk_done, 2 * n + w + 1)
                    act.activation(dst[:, :, :].rearrange("p a t -> p (a t)"),
                                   ps[:, b0:b0 + 2, :].rearrange("p b t -> p (b t)"),
                                   ACT.Copy, scale=sc).then_inc(qk_out, 1)

            def powers(n):
                act.wait_ge(dwm_ready, n + 1)
                for h in range(H):
                    ins = act.activation(dw[:, h, :], dw[:, h, :], ACT.Exp,
                                         bias=cols[:, ds(n, 1), 0, h:h + 1].rearrange("p a h -> p (a h)"))
                ins.then_inc(dw_ready, 1)
                act.wait_ge(ktr_done, n + 1)
                for h in range(H):
                    act.activation(kw[:, 2 * h:2 * h + 2, :].rearrange("p a d -> p (a d)"),
                                   ps[:, h // 2, (h % 2) * HC:(h % 2) * HC + HC], ACT.Copy,
                                   scale=cols[:, ds(n, 1), 3, h:h + 1].rearrange("p a h -> p (a h)")).then_inc(kw_ready, 1)

            def out_high(n, col, width):
                act.wait_ge(htr_done, 1 + n + 1)
                for t in range(KT):
                    ins = act.activation(xh[:, t, ds(col, width)], ps[:, 6 + t // 4, (t % 4) * P:(t % 4) * P + width],
                                         ACT.Copy, scale=vec("c_g", t))
                ins.then_inc(ch_ready, 1)

            def chunk(n, last, nxt):
                act.wait_ge(cup_read, 1 + 8 * n)
                for h in range(H):
                    act.wait_ge(num_done, 4 * n + h + 1)
                    act.activation(iq[:, h, :], bank((7, 3)[h % 2], HC + 1), ACT.Copy,
                                   scale=cols[:, ds(n, 1), 1, h:h + 1].rearrange("p a h -> p (a h)")).then_inc(iq_ready, 1)
                if last is not None:
                    out_high(*last)
                if nxt is not None:
                    act.wait_ge(cup_done, 8 * n + 8)
                    load_v(nxt)
                    keys_queries(nxt)
                    act.wait_ge(cup_read, 1 + 8 * n + 8)
                    load_o(nxt)
                    act.activation(seeds[:, 7:8], seeds[:, 0:1], ACT.Exp)
                    powers(nxt)
                act.wait_ge(var_ready, 4 * n + 4)
                act.activation(st[:, 40:44], st[:, 25:32:2], ACT.Sqrt, bias=vec("eps")).then_inc(sd_ready, 1)

            for j in range(2):
                act.wait_ge(stage_out[j], 16 + 16 * CH * 4)
            act.wait_ge(c_zero, 2)
            load_v(0)
            load_o(0)
            act.wait_ge(acc_free, FREE0["vo1"] + 72)
            keys_queries(0)
            powers(0)
            chunk(0, None, 1)
            with act.Fori(1, CH - 2) as i:
                chunk(i, (i - 1, i * P - P, P), i + 1)
            chunk(CH - 2, (CH - 3, (CH - 3) * P, P), CH - 1)
            act.wait_ge(cup_read, 1 + 8 * (CH - 1))
            act.dma_start(O["c_o"][0], cs[:, :, :, :]).then_inc(c_sent, 16)
            act.wait_ge(c_sent, 16)
            act.dma_start(cs[:, :, :, :], I["c0"]).then_inc(c_swap, 16)
            act.wait_ge(qk_done, 2 * CH)
            act.dma_start(x[:, :, :], xsave).then_inc(x_in, 16)
            chunk(CH - 1, (CH - 2, (CH - 2) * P, P), None)
            out_high(CH - 1, TP, TS)
            act.wait_ge(cup_read, 1 + 8 * CH)
            act.dma_start(O["c_o"][1], cs[:, :, :, :]).then_inc(c_sent, 16)
            act.wait_ge(cl_ready, 1 + CH)
            act.wait_ge(c_sent, 32)
            act.dma_start(praw[:, :, :], I["pT"][1]).then_inc(p_in, 16)
            act.wait_ge(acc_free, FREE0["out1"] + 24)
            norm(3)
            ffn(1)
            ple(1, B1_PLE)
            act.wait_ge(ple_added, 1 + 48)
            for tt in range(NT):
                root(4, tt)
            for tt in range(NT):
                act.wait_ge(xt_ready, 1 + KT * NT * 4 + KT * (tt + 1))
                sl = slice(tt * TW, (tt + 1) * TW)
                act.dma_start(O["yT"][:, :, sl], ybuf[:, :, sl]).then_inc(y_sent, 16)
            act.wait_ge(y_sent, 16 * NT)
            for s_, n_ in ((aconv_sent, 32), (kv_sent, 48), (ah_sent, 16), (cconv_sent, 32), (m_sent, 16)):
                act.wait_ge(s_, n_)


def tiles(v):
    return v.reshape(-1, P).T


def blocks(w):
    n = w.shape[1] // P
    return w.reshape(KT, P, n, P).transpose(2, 1, 0, 3).reshape(n, P, KT * P)


def pairs(w):
    return w.reshape(2, P, 2, 4, P).transpose(2, 1, 3, 0, 4).reshape(2, P, KT * P)


def block_diagonal(w):
    n, b, _ = w.shape
    per = P // b
    out = np.zeros((P, n // per, P), w.dtype)
    for i in range(n):
        t, r = i // per, (i % per) * b
        out[r:r + b, t, r:r + b] = w[i]
    return out


_OUT = {"yT": (P, KT, TOK), "a_conv_o": (P, AT, 6), "a_h_o": (P, 2, AT), "k_o": (P, P + TS), "v_o": (P, P + TS),
        "c_conv_o": (P, KT, 6), "c_o": (2, P, H, 2, HC + 1), "m_o": (H, 2)}


def kernel(x_prompt, x_sample, cache_a_conv, state_a_h, cache_b_k, cache_b_v, cache_c_conv, state_c_C, state_c_n,
           state_c_m, p_prompt, p_sample, norm_mix_g, norm_ffn_g, final_g, ab_w_in, ab_conv_w, ab_conv_b, ab_w_r,
           ab_b_r, ab_w_i, ab_b_i, ab_lambda, ab_sinks, ab_w_out, c_w_in, c_b_gate, c_conv_w, c_conv_b, c_w_q,
           c_w_k, c_norm_g, c_w_out, ffn_w_in, ffn_w_out, ple_w_proj, ple_w_gate):
    import concourse.bacc as bacc
    from concourse.bass_utils import run_bass_kernel_spmd

    f = np.float32
    a = {}

    def feature_major(prompt, sample):
        v = np.concatenate([prompt[0], sample[0]], axis=0)
        return v.T.reshape(-1, P, TOK).transpose(1, 0, 2)

    a["xT"] = feature_major(x_prompt, x_sample)
    a["pT"] = np.stack([feature_major(p_prompt[j], p_sample[j]) for j in range(2)])
    w = np.asarray(ab_w_in[0])
    g, u, q, k, v = np.split(w, [512, 1024, 1536, 1664], axis=1)
    q = q.reshape(D, 2, 4, HD).transpose(0, 2, 1, 3).reshape(D, 512)
    wo = np.asarray(ab_w_out[0])
    wo = np.concatenate([wo[:512], wo[512:].reshape(2, 4, HD, D).transpose(1, 0, 2, 3).reshape(512, D)])
    wc = np.asarray(c_w_in[0])
    gates = np.zeros((D, P), f)
    gates[:, 0:H] = wc[:, 3 * D:3 * D + H]
    gates[:, 32:32 + H] = wc[:, 3 * D + H:]

    def ffn(j):
        wi, wd = np.asarray(ffn_w_in[j]), np.asarray(ffn_w_out[j])
        gate, up = blocks(wi[:, :F_TILES * P]), blocks(wi[:, F_TILES * P:])
        ups = [np.stack([b for t in (2 * c, 2 * c + 1) for b in (gate[t], up[t])]) for c in range(FCH)]
        downs = [pairs(wd[256 * c:256 * (c + 1)]) for c in range(FCH)]
        out = [ups[0]]
        for c in range(FCH - 1):
            out += [ups[c + 1], downs[c]]
        return out + [downs[-1]]

    def ple(j):
        return [pairs(np.asarray(ple_w_proj[j])), blocks(np.asarray(ple_w_gate[j]))]

    a["wstream"] = np.concatenate(
        [blocks(np.concatenate([u, k, v, q, g], axis=1)), blocks(wo)] + ffn(0) + ple(0)
        + [blocks(gates), blocks(wc[:, :D]), np.zeros((1, P, D), f), blocks(wc[:, D:3 * D]),
           blocks(np.asarray(c_w_out[0]))] + ffn(1) + ple(1))
    assert a["wstream"].shape[0] == NBLK
    vecs = np.zeros((P, NVEC), f)

    def put(name, v):
        v = np.asarray(v)
        vecs[:, VEC[name]:VEC[name] + v.shape[1]] = v

    put("g_mix0", tiles(norm_mix_g[0]))
    put("g_ffn0", tiles(norm_ffn_g[0]))
    put("g_mix1", tiles(norm_mix_g[1]))
    put("g_ffn1", tiles(norm_ffn_g[1]))
    put("g_fin", tiles(final_g))
    put("a_w", np.concatenate([tiles(ab_conv_w[0, j]) for j in range(4)], axis=1))
    put("a_b", tiles(ab_conv_b[0]))
    put("b_r", tiles(ab_b_r[0]))
    put("b_i", tiles(ab_b_i[0]))
    put("lam", tiles(ab_lambda[0]))
    put("h0", tiles(state_a_h[0, 0]))
    put("sink", np.broadcast_to(ab_sinks[0], (P, 8)))
    put("c_w", np.concatenate([tiles(c_conv_w[0, j]) for j in range(4)], axis=1))
    put("c_b", tiles(c_conv_b[0]))
    put("c_g", tiles(c_norm_g[0]))
    vecs[0:H, VEC["b_gate"]] = c_b_gate[0, :H]
    vecs[32:32 + H, VEC["b_gate"]] = c_b_gate[0, H:]
    vecs[0:H, VEC["m0"]] = state_c_m[0, 0]
    vecs[:, VEC["eps"]] = EPS
    a["vecs"] = vecs
    a["ones"] = np.ones((P, P), f)
    a["ident"] = np.eye(P, dtype=f)
    a["lbd"] = np.stack([block_diagonal(np.asarray(ab_w_r[0])), block_diagonal(np.asarray(ab_w_i[0]))], axis=1)
    a["cbd"] = np.stack([block_diagonal(np.asarray(c_w_q[0])), block_diagonal(np.asarray(c_w_k[0]))], axis=1)
    a["a_conv"] = cache_a_conv[0, 0].reshape(3, AT, P).transpose(2, 1, 0)
    a["c_conv"] = cache_c_conv[0, 0].reshape(3, KT, P).transpose(2, 1, 0)
    a["kc"] = cache_b_k[0, 0].reshape(P, P).T
    a["vc"] = cache_b_v[0, 0].reshape(P, P)
    c0 = np.asarray(state_c_C[0, 0]).reshape(H, 2, P, HC).transpose(2, 0, 1, 3)
    n0 = np.asarray(state_c_n[0, 0]).reshape(H, 2, P).transpose(2, 0, 1)[..., None]
    a["c0"] = np.concatenate([c0, n0], axis=3)
    qi, kj = np.arange(P)[:, None], np.arange(2 * P)[None, :] - P
    back = qi // 64 - kj // 64
    seen = (back >= 0) & (back <= 2)
    d = np.abs(qi - kj).astype(f)
    far = f(1e30)
    a["dist"] = np.stack([np.where(seen & (kj >= 0), d, far), np.where(seen, d, far), np.where(kj < TS, d, far)],
                         axis=1).astype(f)
    a["sel"] = np.repeat(np.eye(H, dtype=f)[:, :, None], P, axis=2)
    a["cmask"] = np.where(np.arange(P)[:, None] <= np.arange(P)[None, :], f(0), f(NEG)).astype(f)

    nc = bacc.Bacc("TRN2", target_bir_lowering=False, num_devices=1)
    a = {n: np.ascontiguousarray(v, dtype=f) for n, v in a.items()}
    ins = {n: nc.dram_tensor(n, v.shape, F32, kind="ExternalInput").ap() for n, v in a.items()}
    outs = {n: nc.dram_tensor(n, s, F32, kind="ExternalOutput").ap() for n, s in _OUT.items()}
    build(nc, ins, outs)
    r = run_bass_kernel_spmd(nc, [a], core_ids=[0]).results[0]

    y = r["yT"].transpose(1, 0, 2).reshape(D, TOK).T
    a_conv, c_conv = (r[n].transpose(2, 1, 0).reshape(2, 3, -1) for n in ("a_conv_o", "c_conv_o"))
    a_h = r["a_h_o"].transpose(1, 2, 0).reshape(2, -1)
    kk, vv = r["k_o"].T, r["v_o"].T
    c = r["c_o"].transpose(0, 2, 3, 1, 4)
    m = r["m_o"].T
    cc = [c[j, ..., :HC].reshape(1, 1, H, HC, HC) for j in range(2)]
    cn = [c[j, ..., HC].reshape(1, 1, H, HC) for j in range(2)]
    out = []
    for j in range(2):
        rows_ = slice(0, P) if j == 0 else slice(P, P + TS)
        out.append([a_conv[j][None, None], a_h[j][None, None], kk[rows_].reshape(1, 1, -1, 2, HD),
                    vv[rows_].reshape(1, 1, -1, 2, HD), c_conv[j][None, None], cc[j], cn[j], m[j].reshape(1, 1, H)])
    return tuple([y[:TP][None], y[TP:][None]] + out[0] + out[1])
```
